# Optimizing a Trainium2 kernel written in Bass

```python
import math
import jax, jax.numpy as jnp
from jax import lax
import numpy as np

D_MODEL = 1024
BATCH = 1
SEQ = 512
DEPTH = 2
DEC_BATCH = 8
DEC_SEQ = 16
PAST_LEN = 1024

CHUNK = 64
N_HEADS = 16
HEAD_DIM = D_MODEL // N_HEADS
SB_BLOCK = 128
POOL_WINDOWS = (2, 4, 8, 16)
N_POOL_GROUPS = len(POOL_WINDOWS)
POOL_GROUP = D_MODEL // N_POOL_GROUPS
POOL_MAX = max(POOL_WINDOWS)
D_FF = ((8 * D_MODEL // 3 + 255) // 256) * 256
PLE_DIM = 256
N_POOL = (DEPTH + 1) // 2
N_SB = DEPTH // 2
ALPHA = (2.0 * DEPTH) ** 0.25
BETA = (8.0 * DEPTH) ** -0.25
LN_EPS = 1e-5
SB_SCALE = 1.0 / math.sqrt(HEAD_DIM)

kernel_name = "streaming_pool_stickbreak_hybrid"

def layer_norm(x, g, b):
    xf = x.astype(jnp.float32)
    mu = jnp.mean(xf, axis=-1, keepdims=True)
    var = jnp.mean(jnp.square(xf - mu), axis=-1, keepdims=True)
    y = (xf - mu) * lax.rsqrt(var + LN_EPS)
    return (y * g.astype(jnp.float32) + b.astype(jnp.float32)).astype(x.dtype)

def swiglu(x, w1, w3, w2):
    return (jax.nn.silu(x @ w1) * (x @ w3)) @ w2

def pool_mixer(x, prev, pos0, w_grp, scale):
    B, S, D = x.shape
    xe = jnp.concatenate([prev.astype(x.dtype), x], axis=1)
    cs = lax.cumsum(xe.astype(jnp.float32), axis=1)
    cs = jnp.concatenate([jnp.zeros((B, 1, D), jnp.float32), cs], axis=1)
    end = cs[:, POOL_MAX:]
    pos = pos0 + jnp.arange(S)
    outs = []
    for g, w in enumerate(POOL_WINDOWS):
        sl = slice(g * POOL_GROUP, (g + 1) * POOL_GROUP)
        start = cs[:, POOL_MAX - w:POOL_MAX - w + S, sl]
        cnt = jnp.minimum(w, pos + 1).astype(jnp.float32)
        mean = (end[..., sl] - start) / cnt[None, :, None]
        outs.append(mean - x[..., sl].astype(jnp.float32))
    y = jnp.stack(outs, axis=2).astype(x.dtype)
    y = jnp.einsum('bsgc,gcd->bsgd', y, w_grp).reshape(B, S, D) * scale
    new_prev = xe[:, -(POOL_MAX - 1):]
    return y, new_prev

def sb_core(q, k, v, q_pos, k_pos):
    z = jnp.einsum('bqhd,bkhd->bhqk', q, k, preferred_element_type=jnp.float32) * SB_SCALE
    mask = k_pos[None, :] < q_pos[:, None]
    log_keep = jnp.where(mask, jax.nn.log_sigmoid(-z), 0.0)
    after = lax.cumsum(log_keep, axis=3, reverse=True) - log_keep
    w = jnp.where(mask, jnp.exp(jax.nn.log_sigmoid(z) + after), 0.0)
    return jnp.einsum('bhqk,bkhd->bqhd', w.astype(v.dtype), v)

def sb_qkv(x, w_in):
    B, S, _ = x.shape
    qkv = (x @ w_in).reshape(B, S, 3, N_HEADS, HEAD_DIM)
    return qkv[:, :, 0], qkv[:, :, 1], qkv[:, :, 2]

def sb_prompt(x, w_in, w_out):
    B, S, D = x.shape
    q, k, v = sb_qkv(x, w_in)
    nblk = S // SB_BLOCK
    qb = q.reshape(B, nblk, SB_BLOCK, N_HEADS, HEAD_DIM).transpose(1, 0, 2, 3, 4)
    pb = jnp.arange(S).reshape(nblk, SB_BLOCK)
    kpos = jnp.arange(S)
    o = lax.map(lambda a: sb_core(a[0], k, v, a[1], kpos), (qb, pb))
    o = o.transpose(1, 0, 2, 3, 4).reshape(B, S, D)
    return o @ w_out, k, v

def sb_sample(x, k_cache, v_cache, w_in, w_out):
    B, S, D = x.shape
    q, k, v = sb_qkv(x, w_in)
    k_all = jnp.concatenate([k_cache.astype(k.dtype), k], axis=1)
    v_all = jnp.concatenate([v_cache.astype(v.dtype), v], axis=1)
    past = k_cache.shape[1]
    q_pos = past + jnp.arange(S)
    k_pos = jnp.arange(past + S)
    o = sb_core(q, k_all, v_all, q_pos, k_pos).reshape(B, S, D)
    return o @ w_out, k, v

def setup_inputs(seed: int = 0) -> dict:
    key = jax.random.key(seed)
    ks = jax.random.split(key, 20)
    nrm = jax.random.normal
    f32 = jnp.float32
    return {
        "x_prompt": nrm(ks[0], (BATCH, SEQ, D_MODEL), f32),
        "x_sample": nrm(ks[1], (DEC_BATCH, DEC_SEQ, D_MODEL), f32),
        "cache_k": nrm(ks[2], (N_SB, DEC_BATCH, PAST_LEN, N_HEADS, HEAD_DIM), f32),
        "cache_v": nrm(ks[3], (N_SB, DEC_BATCH, PAST_LEN, N_HEADS, HEAD_DIM), f32),
        "state_pool": nrm(ks[4], (N_POOL, DEC_BATCH, POOL_MAX - 1, D_MODEL), f32),
        "p_prompt": nrm(ks[5], (DEPTH, BATCH, SEQ, PLE_DIM), f32),
        "p_sample": nrm(ks[6], (DEPTH, DEC_BATCH, DEC_SEQ, PLE_DIM), f32),
        "ln_g": 1.0 + 0.02 * nrm(ks[7], (DEPTH, 4, D_MODEL), f32),
        "ln_b": 0.02 * nrm(ks[8], (DEPTH, 4, D_MODEL), f32),
        "ffn_w1": nrm(ks[9], (DEPTH, 2, D_MODEL, D_FF), f32) * D_MODEL ** -0.5,
        "ffn_w3": nrm(ks[10], (DEPTH, 2, D_MODEL, D_FF), f32) * D_MODEL ** -0.5,
        "ffn_w2": nrm(ks[11], (DEPTH, 2, D_FF, D_MODEL), f32) * (D_FF ** -0.5 * BETA),
        "pool_w": nrm(ks[12], (N_POOL, N_POOL_GROUPS, POOL_GROUP, POOL_GROUP), f32) * (POOL_GROUP ** -0.5 * BETA),
        "pool_scale": 1.0 + 0.02 * nrm(ks[13], (N_POOL, D_MODEL), f32),
        "sb_w_in": nrm(ks[14], (N_SB, D_MODEL, 3 * D_MODEL), f32) * D_MODEL ** -0.5,
        "sb_w_out": nrm(ks[15], (N_SB, D_MODEL, D_MODEL), f32) * (D_MODEL ** -0.5 * BETA),
        "ple_w_gate": nrm(ks[16], (DEPTH, D_MODEL, D_MODEL), f32) * D_MODEL ** -0.5,
        "ple_b_gate": 0.02 * nrm(ks[17], (DEPTH, D_MODEL), f32),
        "ple_w_proj": nrm(ks[18], (DEPTH, PLE_DIM, D_MODEL), f32) * (PLE_DIM ** -0.5 * BETA),
    }

def reference(x_prompt, x_sample, cache_k, cache_v, state_pool, p_prompt, p_sample,
              ln_g, ln_b, ffn_w1, ffn_w3, ffn_w2, pool_w, pool_scale,
              sb_w_in, sb_w_out, ple_w_gate, ple_b_gate, ple_w_proj):
    def half_ffn(x, i, n):
        h = 0.5 * swiglu(x, ffn_w1[i, n], ffn_w3[i, n], ffn_w2[i, n])
        return layer_norm(ALPHA * x + h, ln_g[i, 2 * n], ln_b[i, 2 * n])

    def post_mixer(x, m, p_i, i):
        x = layer_norm(ALPHA * x + m, ln_g[i, 1], ln_b[i, 1])
        x = half_ffn(x, i, 1)
        gate = jax.nn.sigmoid(x @ ple_w_gate[i] + ple_b_gate[i])
        e = p_i @ ple_w_proj[i]
        return layer_norm(ALPHA * x + gate * e, ln_g[i, 3], ln_b[i, 3])

    xp, xs = x_prompt, x_sample
    kp_l, vp_l, ks_l, vs_l, pp_l, ps_l = [], [], [], [], [], []
    for i in range(DEPTH):
        xp = half_ffn(xp, i, 0)
        xs = half_ffn(xs, i, 0)
        j = i // 2
        if i % 2 == 0:
            prev0 = jnp.zeros((xp.shape[0], POOL_MAX - 1, D_MODEL), xp.dtype)
            mp, np_ = pool_mixer(xp, prev0, 0, pool_w[j], pool_scale[j])
            ms, ns_ = pool_mixer(xs, state_pool[j], state_pool.shape[2] * 0 + PAST_LEN, pool_w[j], pool_scale[j])
            pp_l.append(np_)
            ps_l.append(ns_)
        else:
            mp, kp, vp = sb_prompt(xp, sb_w_in[j], sb_w_out[j])
            ms, kn, vn = sb_sample(xs, cache_k[j], cache_v[j], sb_w_in[j], sb_w_out[j])
            kp_l.append(kp); vp_l.append(vp); ks_l.append(kn); vs_l.append(vn)
        xp = post_mixer(xp, mp, p_prompt[i], i)
        xs = post_mixer(xs, ms, p_sample[i], i)

    new_k_prompt = jnp.stack(kp_l)
    new_v_prompt = jnp.stack(vp_l)
    new_k_sample = jnp.stack(ks_l)
    new_v_sample = jnp.stack(vs_l)
    new_pool_prompt = jnp.stack(pp_l)
    new_pool_sample = jnp.stack(ps_l)
    return (xp, xs, new_k_prompt, new_v_prompt, new_k_sample, new_v_sample, new_pool_prompt, new_pool_sample)


_drawn_inputs = setup_inputs


def setup_inputs(seed=0):
    import zlib

    import numpy as np

    out = dict(_drawn_inputs(seed))
    spreads = {}
    factors = {'pool_scale': 23.673, 'ple_b_gate': 27.28}
    for name, (base, spread) in spreads.items():
        noise = np.random.default_rng([zlib.crc32(name.encode()), seed]).standard_normal(out[name].shape)
        drawn = base * np.exp(spread * noise) if base else spread * noise
        out[name] = __import__('jax').numpy.asarray(drawn.astype(out[name].dtype))
    for name, factor in factors.items():
        out[name] = (out[name] * factor).astype(out[name].dtype)
    return out
```

```python
from contextlib import ExitStack

import concourse.bass as bass
from concourse import mybir

P = 128
D_MODEL = 1024
SEQ = 512
DEPTH = 2
DEC_BATCH = 8
DEC_SEQ = 16
PAST = 1024
HEADS = 16
HEAD_DIM = D_MODEL // HEADS
WINDOWS = (2, 4, 8, 16)
PREV = max(WINDOWS) - 1
D_FF = 2816
PLE = 256
ALPHA = (2.0 * DEPTH) ** 0.25
EPS = 1e-5
SCALE = HEAD_DIM ** -0.5
MASKED = -(2.0 ** 99)

TOKENS = SEQ + DEC_BATCH * DEC_SEQ
TILES = TOKENS // P
PROMPT_TILES = SEQ // P
HALF = TOKENS // 2
DC = D_MODEL // P
FC = D_FF // P
FH = FC // 2
PAIRS = HEADS // 2
SLOT = 12
EXT = PREV + SEQ + DEC_BATCH * (PREV + DEC_SEQ)
SEG = PREV + DEC_SEQ
KEY_BLOCKS = PAST // P

F32 = mybir.dt.float32
F32R = mybir.dt.float32r
I32 = mybir.dt.int32
SIGN = -(1 << 31)
ALU = mybir.AluOpType
ACT = mybir.ActivationFunctionType

UNITS = [("p", 0, 0), ("p", 1, 0), ("s", 0), ("p", 0, 1), ("s", 1), ("p", 1, 1), ("s", 2), ("p", 0, 2), ("s", 3),
         ("p", 1, 2)]
NU = len(UNITS)
SAMPLE_AT = [u for u, unit in enumerate(UNITS) if unit[0] == "s"]
PART_AT = (0, 512, 896)
PART_COLS = (512, 384, 512)
AUX = 13
RSTEPS = KEY_BLOCKS + 1


class Stage:

    def __init__(self, kind, chunks=(0, 0), what="", layer=0, n=0, half=0, pairs=0, then=""):
        self.kind, self.chunks, self.what, self.layer = kind, chunks, what, layer
        self.n, self.half, self.pairs, self.then = n, half, pairs, then
        self.base = {}
        self.landed = 0
        self.after = None


def plan_stages():
    stages = []

    def add(kind, chunks=(0, 0), **more):
        stages.append(Stage(kind, chunks, **more))

    def ffn(layer, n):
        for half in range(2):
            add("pair", (DC, DC), pairs=FH, what="ffn", layer=layer, n=n, half=half)
            add("tile", (FH, FH), what="down", layer=layer, n=n, half=half)

    add("norm", what="load", then="split", layer=0, n=0)
    for layer in range(DEPTH):
        pool = layer % 2 == 0
        last = layer == DEPTH - 1
        ffn(layer, 0)
        add("norm", what="norm", layer=layer, n=0, then="window" if pool else "split")
        if pool:
            add("window", layer=layer)
            add("tile", (2, 2), what="pool", layer=layer, half=0)
        else:
            add("attention", (SLOT, SLOT), layer=layer)
            add("tile", (DC, DC), what="out", layer=layer, half=0)
        add("norm", what="norm", layer=layer, n=1, then="split")
        ffn(layer, 1)
        add("norm", what="norm", layer=layer, n=2, then="split")
        add("ple", layer=layer)
        add("pair", (DC, PLE // P), pairs=DC, what="ple", layer=layer)
        add("norm", what="norm", layer=layer, n=3, then="none" if last else "split")

    value = {}
    for st in stages:
        st.base = {k: value.get(k, 0) for k in NAMES}
        for k, v in increments(st).items():
            value[k] = value.get(k, 0) + v
    for st, nxt in zip(stages, stages[1:] + [None]):
        after = [s for s in stages[stages.index(st) + 1:] if s.chunks[0]]
        st.after = after[0].chunks if after else None
    return stages


def after(engine, semaphore, value):
    if value:
        engine.wait_ge(semaphore, value)


NAMES = ["w", "gate_full", "up_full", "act_done", "prod_done", "h_hi", "h_lo", "acc_full", "evac_act", "evac_dve",
         "yt_full", "res_done", "stat", "std", "x_norm", "xt_full", "x_hi", "x_lo", "gb", "d_done", "d_hi", "d_lo",
         "pt_full", "pt_hi", "pt_lo", "state"]


def increments(st):
    if st.kind == "pair":
        n = dict.fromkeys(["gate_full", "up_full", "act_done", "prod_done"], st.pairs)
        if st.what == "ffn":
            n.update(h_hi=st.pairs, h_lo=st.pairs)
        return n | {"w": 2 * st.pairs}
    if st.kind == "tile":
        return {"w": DC, "acc_full": DC, ("evac_dve" if st.half else "evac_act"): DC}
    if st.kind == "norm":
        n = {}
        if st.what == "norm":
            n = dict.fromkeys(["yt_full", "res_done", "stat", "std", "x_norm"], TILES) | {"gb": 32}
        if st.then != "none":
            n.update(xt_full=TILES, x_hi=TILES)
        if st.then == "split":
            n.update(x_lo=TILES)
        return n
    if st.kind == "window":
        return {"d_done": DC, "d_hi": DC, "d_lo": DC, "state": 16}
    if st.kind == "ple":
        return {"pt_full": 2, "pt_hi": 2, "pt_lo": 2}
    if st.kind == "attention":
        return {"w": 2 * PAIRS, "x_hi": DC, "x_lo": DC}
    raise ValueError(st.kind)


def streaming_trunk(nc, x_prompt, x_sample, cache_k, cache_v, state_pool, p_prompt, p_sample, ln_g, ln_b, ffn_w1,
                    ffn_w3, ffn_w2, pool_w, pool_scale, sb_w_in, sb_w_out, ple_w_gate, ple_b_gate, ple_w_proj,
                    y_prompt, y_sample, new_k_prompt, new_v_prompt, new_k_sample, new_v_sample, new_pool_prompt,
                    new_pool_sample):
    stages = plan_stages()
    attention = next(s for s in stages if s.kind == "attention")
    norms = [s for s in stages if s.kind == "norm" and s.what == "norm"]

    with ExitStack() as ctx:
        def sb(name, shape, dt=F32):
            return ctx.enter_context(nc.sbuf_tensor(name, shape, dt))

        def sem(name):
            return ctx.enter_context(nc.semaphore(name))

        x = sb("x", [P, TILES, D_MODEL])
        y_t = sb("y_t", [P, DC, TOKENS])
        w_raw = sb("w_raw", [P, 2, SLOT, P])
        w_hi = sb("w_hi", [P, 2, SLOT, P], F32R)
        w_lo = sb("w_lo", [P, 2, SLOT, P], F32R)
        act = sb("act", [P, TOKENS])
        ident = sb("ident", [P, P])
        ident_r = sb("ident_r", [P, P], F32R)
        neg_tri = sb("neg_tri", [P, P])
        neg_ones = sb("neg_ones", [P, P])
        mask_f = sb("mask_f", [P, 2, P])
        mask_r = sb("mask_r", [P, 2, P], F32R)
        rcp = sb("rcp", [P, PREV])
        eps = sb("eps", [P, 1])
        zero = sb("zero", [P, 2, DEC_SEQ])
        stats = sb("stats", [P, TILES, 12])
        mv = sb("mv", [P, TILES, 2])
        std = sb("std", [P, TILES])
        rstd = sb("rstd", [P, TILES])
        gate_b = sb("gate_b", [P, DEPTH, DC])
        scale_p = sb("scale_p", [P, DC])

        at_xt = ctx.enter_context(nc.sbuf_tensor("region_xt", [P, 2 * DC * TOKENS], F32))
        at_gb = ctx.enter_context(nc.sbuf_tensor("region_gb", [P, 2 * D_MODEL], F32))
        arena_bytes = 75776
        at_arena = ctx.enter_context(nc.sbuf_tensor("region_arena", [P, arena_bytes // 4], F32))
        sizes = {at_xt.name: 8 * DC * TOKENS, at_gb.name: 8 * D_MODEL, at_arena.name: arena_bytes}
        used = {}

        def place(where, name, shape, dt=F32, at=None):
            nbytes = 4
            for n in shape[1:]:
                nbytes *= n
            start = used.get(where.name, 0) if at is None else at
            used[where.name] = start + nbytes
            assert used[where.name] <= sizes[where.name], (name, used[where.name], sizes[where.name])
            base = nc.lookup_mls(where.name).memorylocations[0].addr
            return nc.alloc_sbuf_tensor_at(name, shape, dt, offset=base + start)

        xt_hi = place(at_xt, "xt_hi", [P, DC, TOKENS], F32R)
        xt_lo = place(at_xt, "xt_lo", [P, DC, TOKENS], F32R)
        ext = place(at_xt, "ext", [P, DC, EXT], at=0)
        state_t = place(at_xt, "state_t", [DEC_BATCH * PREV, D_MODEL])
        win = [place(at_xt, f"win{n}", [P, EXT + 1]) for n in range(2)]

        g_b = place(at_gb, "g_b", [P, D_MODEL])
        b_b = place(at_gb, "b_b", [P, D_MODEL])
        q_t = place(at_gb, "q_t", [P, TOKENS], at=0)
        k_t = place(at_gb, "k_t", [P, TOKENS])
        k_tok = place(at_gb, "k_tok", [P, TILES, P])

        h_hi = place(at_arena, "h_hi", [P, FH, TOKENS], F32R)
        h_lo = place(at_arena, "h_lo", [P, FH, TOKENS], F32R)
        p_tok = place(at_arena, "p_tok", [P, TILES, PLE])
        p_hi = place(at_arena, "p_hi", [P, PLE // P, TOKENS], F32R)
        p_lo = place(at_arena, "p_lo", [P, PLE // P, TOKENS], F32R)
        k_raw = place(at_arena, "k_raw", [P, 2, 2, KEY_BLOCKS, P], at=0)
        v_raw = place(at_arena, "v_raw", [P, 2, 2, KEY_BLOCKS, P])
        kc_t = place(at_arena, "kc_t", [P, 2, KEY_BLOCKS, P])
        sp_p = place(at_arena, "sp_p", [P, 2, sum(PART_COLS)])
        sp_s = place(at_arena, "sp_s", [P, 2, 2, KEY_BLOCKS, 2, DEC_SEQ])
        r_sum = place(at_arena, "r_sum", [P, 2, 2, KEY_BLOCKS, 2, DEC_SEQ])
        e_buf = place(at_arena, "e_buf", [P, 2, 512])
        wt = place(at_arena, "wt", [P, 2, 512])
        q_blk = place(at_arena, "q_blk", [P, DEC_BATCH, 2, DEC_SEQ])
        v_tok = place(at_arena, "v_tok", [P, TILES, P])
        v_t = act
        o_t = y_t
        ps = ctx.enter_context(nc.psum_tensor("ps", [P, 8, 512], F32))

        const_step = sem("const_step")
        const_r = sem("const_r")
        x_loaded = sem("x_loaded")
        small_loaded = sem("small_loaded")
        w_loaded = [sem("w_loaded0"), sem("w_loaded1")]
        w_hi_done = sem("w_hi_done")
        w_split = sem("w_split")
        gate_full = sem("gate_full")
        up_full = sem("up_full")
        act_done = sem("act_done")
        prod_done = sem("prod_done")
        h_hi_done = sem("h_hi_done")
        h_lo_done = sem("h_lo_done")
        acc_full = sem("acc_full")
        evac_act = sem("evac_act")
        evac_dve = sem("evac_dve")
        yt_full = sem("yt_full")
        res_done = sem("res_done")
        stat_done = sem("stat_done")
        std_done = sem("std_done")
        x_norm = sem("x_norm")
        xt_full = sem("xt_full")
        x_hi_done = sem("x_hi_done")
        x_lo_done = sem("x_lo_done")
        gb_loaded = sem("gb_loaded")
        dve_step = sem("dve_step")
        state_loaded = sem("state_loaded")
        state_full = sem("state_full")
        state_done = sem("state_done")
        ext_zero = sem("ext_zero")
        d_done = sem("d_done")
        d_hi_done = sem("d_hi_done")
        d_lo_done = sem("d_lo_done")
        p_loaded = sem("p_loaded")
        pt_full = sem("pt_full")
        pt_hi_done = sem("pt_hi_done")
        pt_lo_done = sem("pt_lo_done")
        k_loaded = [sem("k_loaded0"), sem("k_loaded1")]
        v_loaded = [sem("v_loaded0"), sem("v_loaded1")]
        aux_full = [sem("aux_full_a"), sem("aux_full_v")]
        aux_free = [sem("aux_free_a"), sem("aux_free_v")]
        q_blk_zero = sem("q_blk_zero")
        q_blk_done = sem("q_blk_done")
        z_full = sem("z_full")
        na_done = sem("na_done")
        el_done = sem("el_done")
        sp_done = sem("sp_done")
        r_step = sem("r_step")
        s_full = sem("s_full")
        wt_done = sem("wt_done")
        pv_done = sem("pv_done")
        ot_act = sem("ot_act")
        ot_dve = sem("ot_dve")
        kv_stored = sem("kv_stored")
        pool_stored = sem("pool_stored")
        y_stored = sem("y_stored")

        xp = x_prompt[0].rearrange("(t p) d -> p t d", p=P)
        xs = x_sample.rearrange("b s d -> (b s) d")

        def block_source(st, s, i):
            if st.kind == "pair" and st.what == "ffn":
                w = (ffn_w1, ffn_w3)[s][st.layer, st.n].rearrange("(c p) f -> p c f", p=P)
                return [(0, DC, w[:, :, bass.ds(i * P + st.half * FH * P, P)])]
            if st.kind == "pair":
                w = (ple_w_gate, ple_w_proj)[s][st.layer].rearrange("(c p) f -> p c f", p=P)
                return [(0, st.chunks[s], w[:, :, bass.ds(i * P, P)])]
            if st.kind == "tile" and st.what == "down":
                w = ffn_w2[st.layer, st.n].rearrange("(c p) f -> p c f", p=P)
                return [(0, FH, w[:, st.half * FH:(st.half + 1) * FH, bass.ds(i * 2 * P + s * P, P)])]
            if st.kind == "tile" and st.what == "out":
                w = sb_w_out[0].rearrange("(c p) f -> p c f", p=P)
                return [(0, DC, w[:, :, bass.ds(i * 2 * P + s * P, P)])]
            if st.kind == "tile":
                w = pool_w[0].rearrange("g (c p) f -> p g c f", p=P)
                return [(0, 2, w[:, i, :, s * P:(s + 1) * P])]
            w = sb_w_in[0].rearrange("(c p) (m f) -> p c m f", p=P, m=3)
            col = bass.ds(i * P, P)
            if s == 0:
                return [(0, DC, w[:, :, 0, col]), (DC, 4, w[:, 0:4, 2, col])]
            return [(0, 4, w[:, 4:8, 2, col]), (4, DC, w[:, :, 1, col])]

        def block_loads(st):
            return 32 if st.kind == "attention" else 16

        def iterations(st):
            return st.pairs if st.kind == "pair" else PAIRS if st.kind == "attention" else DC // 2

        landed = 0
        for st in stages:
            if st.chunks[0]:
                st.landed = landed
                landed += block_loads(st) * iterations(st)

        def after_stage(st):
            later = [s for s in stages[stages.index(st) + 1:] if s.chunks[0]]
            return later[0] if later else None

        kc = cache_k[0].rearrange("b (k p) h d -> p b k (h d)", p=P)
        vc = cache_v[0].rearrange("b (k p) h d -> p b k (h d)", p=P)

        def attend_pool(pool, st):
            after(pool, evac_dve, st.base["evac_dve"])
            pool.memset(q_blk[:], 0.0).then_inc(q_blk_zero, 1)
            k_out = new_k_prompt[0, 0].rearrange("(t p) h d -> p t (h d)", p=P)
            v_out = new_v_prompt[0, 0].rearrange("(t p) h d -> p t (h d)", p=P)
            ks_out = new_k_sample[0].rearrange("b s h d -> (b s) (h d)")
            vs_out = new_v_sample[0].rearrange("b s h d -> (b s) (h d)")
            with pool.Fori(0, PAIRS) as i:
                col = bass.ds(i * P, P)
                pool.wait_ge(aux_free[0], AUX * i + 5)
                pool.wait_ge(aux_free[1], AUX * i + 5)
                pool.dma_start(k_out[:, :, col], k_tok[:, 0:PROMPT_TILES, :]).then_inc(kv_stored, 16)
                pool.dma_start(ks_out[:, col], k_tok[:, PROMPT_TILES, :]).then_inc(kv_stored, 16)
                pool.dma_start(v_out[:, :, col], v_tok[:, 0:PROMPT_TILES, :]).then_inc(kv_stored, 16)
                pool.dma_start(vs_out[:, col], v_tok[:, PROMPT_TILES, :]).then_inc(kv_stored, 16)
                for su in range(4):
                    slot = su % 2
                    at = i * 4 * RSTEPS + su * RSTEPS
                    pool.wait_ge(sp_done, NU * i + SAMPLE_AT[su] + 1)
                    for h in range(2):
                        own = sp_p[:, h, 384 + 2 * su * DEC_SEQ:384 + 2 * (su + 1) * DEC_SEQ]
                        pool.tensor_tensor(r_sum[:, slot, :, KEY_BLOCKS - 1, h, :],
                                           own.rearrange("p (b s) -> p b s", s=DEC_SEQ), zero[:, :, :],
                                           ALU.add).then_inc(r_step, 1)
                    for n, kb in enumerate(range(KEY_BLOCKS - 2, -1, -1)):
                        pool.wait_ge(r_step, at + 2 + n)
                        pool.tensor_tensor(r_sum[:, slot, :, kb], r_sum[:, slot, :, kb + 1],
                                           sp_s[:, slot, :, kb + 1], ALU.add).then_inc(r_step, 1)

        def cols_of(u):
            return PART_COLS[UNITS[u][2]] if UNITS[u][0] == "p" else 512

        def attend(pe, st, products, moving):
            b = st.base

            def mm(out, w, xx, start=False):
                return pe.matmul(out, w, xx, start=start, stop=True, skip_group_check=True)

            def pair_of_heads(i, begun):
                use = [0, 0]

                def aux_wait(which):
                    if begun or use[which]:
                        pe.wait_ge(aux_free[which], AUX * i + use[which])
                    use[which] += 1

                def project(parts):
                    aux_wait(0)
                    aux_wait(1)
                    for n, (s, chunks) in enumerate(parts):
                        for half in range(2):
                            ins = products(s, chunks, moving(xt_hi), moving(xt_lo), (6, 7), first=(n == 0),
                                           last=(n == len(parts) - 1), only=(half,))
                            if n == len(parts) - 1:
                                ins.then_inc(aux_full[half], 1)
                    return ins

                pe.wait_ge(w_split, b["w"] + 2 * i + 1)
                project([(0, [(c, c) for c in range(8)])])
                pe.wait_ge(w_split, b["w"] + 2 * i + 2)
                project([(0, [(8 + c, c) for c in range(4)]), (1, [(c, 4 + c) for c in range(4)])])
                project([(1, [(4 + c, c) for c in range(8)])])

                def to_tokens(src, uses):
                    for which in range(2):
                        pe.wait_ge(aux_free[which], AUX * i + uses)
                    aux_wait(0)
                    for t in range(PROMPT_TILES):
                        ins = pe.transpose(ps[:, 6, t * P:(t + 1) * P], src[:, t * P:(t + 1) * P], ident[:])
                    ins.then_inc(aux_full[0], 1)
                    aux_wait(1)
                    pe.transpose(ps[:, 7, 0:P], src[:, SEQ:], ident[:]).then_inc(aux_full[1], 1)

                to_tokens(v_t, 2)
                to_tokens(k_t, 3)

                def cached_keys(su):
                    slot = su % 2
                    pe.wait_ge(k_loaded[slot], 64 * i + 32 * (su // 2) + 32)
                    for b2 in range(2):
                        for which in range(2):
                            aux_wait(which)
                            for j in range(4):
                                ins = pe.transpose(ps[:, 6 + which, j * P:(j + 1) * P],
                                                   k_raw[:, slot, b2, 4 * which + j, :], ident[:])
                            ins.then_inc(aux_full[which], 1)

                def scores(u):
                    if u >= 4:
                        pe.wait_ge(wt_done, NU * i + u - 3)
                    z = ps[:, u % 4, :]
                    if UNITS[u][0] == "p":
                        _, h, part = UNITS[u]
                        rows = slice(HEAD_DIM * h, HEAD_DIM * (h + 1))
                        blocks = {0: [(3, 0, 0), (2, P, 0), (4, 3 * P, 1)], 1: [(1, 0, 0)], 2: [(0, 0, 0)]}[part]
                        first = True
                        for kb, at, mask in blocks:
                            stop = TOKENS if kb == 4 else SEQ
                            n = stop - kb * P
                            mm(z[:, at:at + n], k_t[rows, kb * P:(kb + 1) * P], q_t[rows, kb * P:stop], start=first)
                            ins = mm(z[:, at:at + P], ident_r[:], mask_r[:, mask, :])
                            first = False
                    else:
                        su = UNITS[u][1]
                        pe.wait_ge(q_blk_done, 2 * i + 2)
                        for which in range(2):
                            pe.wait_ge(aux_free[which], AUX * i + 5 + 2 * su + 2)
                        first = True
                        for b2 in range(2):
                            for kb in range(KEY_BLOCKS):
                                at = (b2 * KEY_BLOCKS + kb) * 2 * DEC_SEQ
                                ins = mm(z[:, at:at + 2 * DEC_SEQ], kc_t[:, b2, kb, :],
                                         q_blk[:, 2 * su + b2].rearrange("p h s -> p (h s)"), start=first)
                                first = False
                    ins.then_inc(z_full, 1)

                def suffix(u):
                    pe.wait_ge(sp_done, NU * i + u + 1)
                    z = ps[:, u % 4, :]
                    if UNITS[u][0] == "p":
                        _, h, part = UNITS[u]
                        sp = sp_p[:, h, :]
                        at, n = PART_AT[part], PART_COLS[part]
                        ins = mm(z[:, 0:n], neg_tri[:], sp[:, at:at + n])
                        kb3, kb2, kb1 = sp[:, 0:P], sp[:, P:3 * P], sp[:, 512:896]
                        later = {0: [(2 * P, 3 * P, kb3)], 1: [(P, 3 * P, kb2), (2 * P, 3 * P, kb3)],
                                 2: [(P, 4 * P, kb1), (2 * P, 4 * P, kb2), (3 * P, 4 * P, kb3)]}[part]
                        for lo, hi, src in later:
                            ins = mm(z[:, lo:hi], neg_ones[:], src)
                    else:
                        su = UNITS[u][1]
                        mm(z, neg_tri[:], sp_s[:, su % 2].rearrange("p b k h s -> p (b k h s)"))
                        pe.wait_ge(r_step, i * 4 * RSTEPS + (su + 1) * RSTEPS)
                        ins = mm(z, neg_ones[:], r_sum[:, su % 2].rearrange("p b k h s -> p (b k h s)"))
                    ins.then_inc(s_full, 1)

                def values(u):
                    pe.wait_ge(wt_done, NU * i + u + 1)
                    if u == 0:
                        for which in range(2):
                            pe.wait_ge(aux_free[which], AUX * i + 4)
                        if begun:
                            pe.wait_ge(ot_dve, i)
                    w = wt[:, u % 2, :]
                    if UNITS[u][0] == "p":
                        _, h, part = UNITS[u]
                        rows = slice(HEAD_DIM * h, HEAD_DIM * (h + 1))
                        v = lambda kb: v_tok[:, kb, rows]
                        if part == 0:
                            mm(ps[rows, 4, 3 * P:4 * P], v(3), w[:, 0:P], start=True)
                            mm(ps[rows, 4, 2 * P:4 * P], v(2), w[:, P:3 * P])
                            ins = mm(ps[rows, 5, 0:P], v(4), w[:, 3 * P:4 * P], start=True)
                        elif part == 1:
                            ins = mm(ps[rows, 4, P:4 * P], v(1), w[:, 0:3 * P])
                        else:
                            ins = mm(ps[rows, 4, :], v(0), w)
                    else:
                        su = UNITS[u][1]
                        slot = su % 2
                        pe.wait_ge(v_loaded[slot], 64 * i + 32 * (su // 2) + 32)
                        for b2 in range(2):
                            out = ps[:, 5, P + (2 * su + b2) * 2 * DEC_SEQ:P + (2 * su + b2 + 1) * 2 * DEC_SEQ]
                            for kb in range(KEY_BLOCKS):
                                at = (b2 * KEY_BLOCKS + kb) * 2 * DEC_SEQ
                                ins = mm(out, v_raw[:, slot, b2, kb, :], w[:, at:at + 2 * DEC_SEQ])
                    ins.then_inc(pv_done, 1)

                for u in range(NU + 2):
                    if u < NU:
                        if u == 0:
                            for which in range(2):
                                pe.wait_ge(aux_free[which], AUX * i + 3)
                        scores(u)
                    if u + 1 in SAMPLE_AT:
                        cached_keys(SAMPLE_AT.index(u + 1))
                    if 1 <= u <= NU:
                        suffix(u - 1)
                    if u >= 2:
                        values(u - 2)

            pair_of_heads(0, False)
            with pe.Fori(1, PAIRS) as i:
                pair_of_heads(i, True)


        block = ctx.enter_context(nc.Block())

        @block.sync
        def _(sp):
            for t in range(PROMPT_TILES):
                sp.dma_start(x[:, t, :], xp[:, t, :]).then_inc(x_loaded, 16)
            sp.dma_start(x[:, PROMPT_TILES, :], xs).then_inc(x_loaded, 16)

            def load_blocks(st, i, wait=True):
                for s in range(2):
                    if wait:
                        sp.wait_ge(w_split, st.base["w"] + 2 * i + s - 1)
                    for c0, n, src in block_source(st, s, i):
                        sp.dma_start(w_raw[:, s, c0:c0 + n, :], src).then_inc(w_loaded[s], 16)

            def load_cache(i, su):
                col = bass.ds(i * P, P)
                slot = su % 2
                if su >= 2:
                    sp.wait_ge(aux_full[1], AUX * i + 5 + 2 * (su - 1))
                elif not isinstance(i, int):
                    sp.wait_ge(aux_full[1], AUX * i - AUX + 5 + 2 * (su + 3))
                for b in range(2):
                    sp.dma_start(k_raw[:, slot, b], kc[:, 2 * su + b, :, col]).then_inc(k_loaded[slot], 16)
                if su >= 2:
                    sp.wait_ge(pv_done, NU * i + SAMPLE_AT[su - 2] + 1)
                elif not isinstance(i, int):
                    sp.wait_ge(pv_done, NU * i - NU + SAMPLE_AT[su + 2] + 1)
                for b in range(2):
                    sp.dma_start(v_raw[:, slot, b], vc[:, 2 * su + b, :, col]).then_inc(v_loaded[slot], 16)

            for st in stages:
                if not st.chunks[0]:
                    continue
                if st.kind != "attention":
                    if st.base["w"] == 0:
                        load_blocks(st, 0, wait=False)
                    with sp.Fori(1 if st.base["w"] == 0 else 0, iterations(st)) as i:
                        load_blocks(st, i)
                    continue
                load_blocks(st, 0)
                after(sp, evac_dve, st.base["evac_dve"])
                for su in range(4):
                    load_cache(0, su)
                with sp.Fori(1, PAIRS) as i:
                    load_blocks(st, i)
                    for su in range(4):
                        load_cache(i, su)

        @block.gpsimd
        def _(pool):
            step = [0]

            def link(ins):
                step[0] += 1
                ins.then_inc(const_step, 1)
                pool.wait_ge(const_step, step[0])

            pool.dma_start(gate_b[:, :, :], ple_b_gate.rearrange("l (c p) -> p l c", p=P),
                           allow_slow_non_contiguous=True).then_inc(small_loaded, 16)
            pool.dma_start(scale_p[:, :], pool_scale[0].rearrange("(c p) -> p c", p=P),
                           allow_slow_non_contiguous=True).then_inc(small_loaded, 16)

            def load_gb(st):
                for dst, src in ((g_b, ln_g), (b_b, ln_b)):
                    row = src[st.layer, st.n:st.n + 1, :]
                    pool.dma_start(dst[:, :], row.broadcast_to([P, D_MODEL])).then_inc(gb_loaded, 16)

            def load_p(layer):
                pool.dma_start(p_tok[:, 0:PROMPT_TILES, :],
                               p_prompt[layer, 0].rearrange("(t p) d -> p t d", p=P)).then_inc(p_loaded, 16)
                pool.dma_start(p_tok[:, PROMPT_TILES, :],
                               p_sample[layer].rearrange("b s d -> (b s) d")).then_inc(p_loaded, 16)

            load_gb(norms[0])
            load_p(0)
            pool.memset(ident[:], 0.0)
            pool.memset(neg_tri[:], -1.0)
            pool.memset(neg_ones[:], -1.0)
            pool.memset(eps[:], EPS)
            pool.memset(zero[:], 0.0)
            for t in range(PREV):
                pool.memset(rcp[:, t:t + 1], 1.0 / (t + 1))
            link(pool.memset(mask_f[:], 0.0))
            link(pool.affine_select(out=ident[:], in_=ident[:], compare_op=ALU.not_equal, fill=1.0, base=0,
                                    pattern=[[-1, P]], channel_multiplier=1))
            link(pool.affine_select(out=neg_tri[:], in_=neg_tri[:], compare_op=ALU.is_ge, fill=0.0, base=0,
                                    pattern=[[-1, P]], channel_multiplier=1))
            link(pool.affine_select(out=mask_f[:], in_=mask_f[:], compare_op=ALU.is_gt, fill=MASKED, base=0,
                                    pattern=[[0, 2], [1, P]], channel_multiplier=-1))
            own = mask_f[:, 1, :].rearrange("p (b s) -> p b s", s=DEC_SEQ)
            link(pool.affine_select(out=own, in_=own, compare_op=ALU.is_ge, fill=MASKED, base=0,
                                    pattern=[[-DEC_SEQ, DEC_BATCH], [0, DEC_SEQ]], channel_multiplier=1))

            norm_index = 0
            for st in stages:
                b = st.base
                if st.kind == "norm" and st.what == "norm":
                    norm_index += 1
                    pool.wait_ge(x_norm, b["x_norm"] + TILES)
                    if norm_index < len(norms) and norms[norm_index].base["w"] <= attention.base["w"]:
                        load_gb(norms[norm_index])
                    elif norm_index < len(norms) and st.base["w"] > attention.base["w"]:
                        load_gb(norms[norm_index])
                    if st.then == "window":
                        pool.dma_start(new_pool_prompt[0, 0], x[P - PREV:P, PROMPT_TILES - 1, :]).then_inc(pool_stored, 16)
                        for n in range(DEC_BATCH):
                            lo = (n + 1) * DEC_SEQ - PREV
                            pool.dma_start(new_pool_sample[0, n], x[lo:lo + PREV, PROMPT_TILES, :]).then_inc(pool_stored, 16)
                    if st.then == "none":
                        pool.dma_start(y_prompt[0].rearrange("(t p) d -> p t d", p=P),
                                       x[:, 0:PROMPT_TILES, :]).then_inc(y_stored, 16)
                        pool.dma_start(y_sample.rearrange("b s d -> (b s) d"),
                                       x[:, PROMPT_TILES, :]).then_inc(y_stored, 16)
                if st.kind == "tile" and st.what == "down" and st.half == 1 and st.layer == 0 and st.n == 0:
                    after(pool, up_full, b["up_full"])
                    pool.dma_start(state_t[:, :], state_pool[0].rearrange("b r d -> (b r) d")).then_inc(state_loaded, 16)
                    pool.memset(ext[:, :, 0:PREV], 0.0).then_inc(ext_zero, 1)
                if st.kind == "attention":
                    attend_pool(pool, st)
                    pool.wait_ge(kv_stored, 64 * PAIRS)
                    pool.wait_ge(r_step, 4 * RSTEPS * PAIRS)
                    pool.wait_ge(ot_dve, PAIRS)
                    load_gb(norms[norm_index])
                    load_p(1)
            pool.wait_ge(pool_stored, 16 * (1 + DEC_BATCH))
            pool.wait_ge(kv_stored, 64 * PAIRS)
            pool.wait_ge(y_stored, 32)

        @block.scalar
        def _(se):
            def cvt(st, n, s, landed_at):
                k = st.chunks[s]
                se.wait_ge(w_loaded[s], landed_at)
                se.activation(w_hi[:, s, 0:k, :], w_raw[:, s, 0:k, :], ACT.Copy).then_inc(w_hi_done, 1)

            def cvt_of(st, i, s):
                cvt(st, None, s, st.landed + block_loads(st) * (i + 1))

            def next_cvt(st, i, s, last):
                if not last:
                    cvt_of(st, i + 1, s)
                elif after_stage(st) is not None:
                    cvt_of(after_stage(st), 0, s)

            first = next(s for s in stages if s.chunks[0])

            for st in stages:
                b = st.base
                if st.kind == "norm":
                    for t in range(TILES + 1):
                        if t < TILES and st.what == "norm":
                            se.wait_ge(stat_done, b["stat"] + t + 1)
                            se.activation(std[:, t:t + 1], mv[:, t, 1:2], ACT.Sqrt, bias=eps[:, 0:1]).then_inc(std_done, 1)
                        if t >= 1 and st.then != "none":
                            n = t - 1
                            bank = 4 + 2 * (n % 2)
                            se.wait_ge(xt_full, b["xt_full"] + n + 1)
                            tile = ps[:, bank:bank + 2, :].rearrange("p b n -> p (b n)")
                            if st.then == "split":
                                se.activation(xt_hi[:, :, n * P:(n + 1) * P],
                                              tile.rearrange("p (c t) -> p c t", t=P), ACT.Copy).then_inc(x_hi_done, 1)
                            elif n < PROMPT_TILES:
                                se.activation(ext[:, :, PREV + n * P:PREV + (n + 1) * P],
                                              tile.rearrange("p (c t) -> p c t", t=P), ACT.Copy).then_inc(x_hi_done, 1)
                            else:
                                for q in range(2):
                                    cc = slice(4 * q, 4 * q + 4)
                                    own = ext[:, cc, PREV + SEQ:].rearrange("p c (b s) -> p c b s", s=SEG)
                                    ins = se.activation(own[:, :, :, PREV:],
                                                        ps[:, bank + q, :].rearrange("p (c b s) -> p c b s", c=4, s=DEC_SEQ),
                                                        ACT.Copy)
                                ins.then_inc(x_hi_done, 1)
                    if st is stages[0]:
                        cvt_of(first, 0, 0)
                        cvt_of(first, 0, 1)
                elif st.kind == "window":
                    se.wait_ge(state_full, 1)
                    for q in range(2):
                        own = ext[:, 4 * q:4 * q + 4, PREV + SEQ:].rearrange("p c (b s) -> p c b s", s=SEG)
                        src = ps[:, q, :].rearrange("p (c r) -> p c r", c=4)[:, :, 0:DEC_BATCH * PREV]
                        ins = se.activation(own[:, :, :, 0:PREV], src.rearrange("p c (b s) -> p c b s", s=PREV), ACT.Copy)
                    ins.then_inc(state_done, 1)
                    for c in range(DC):
                        se.wait_ge(d_done, b["d_done"] + c + 1)
                        se.activation(h_hi[:, c, 0:SEQ], ext[:, c, PREV:PREV + SEQ], ACT.Copy)
                        own = ext[:, c, PREV + SEQ:].rearrange("p (b s) -> p b s", s=SEG)
                        se.activation(h_hi[:, c, SEQ:].rearrange("p (b s) -> p b s", s=DEC_SEQ), own[:, :, PREV:],
                                      ACT.Copy).then_inc(d_hi_done, 1)
                elif st.kind == "ple":
                    for c in range(PLE // P):
                        se.wait_ge(pt_full, b["pt_full"] + c + 1)
                        se.activation(p_hi[:, c, :], ps[:, 4 + 2 * c:6 + 2 * c, :].rearrange("p b n -> p (b n)")[:, 0:TOKENS],
                                      ACT.Copy).then_inc(pt_hi_done, 1)
                elif st.kind == "pair":
                    def pair(i, last):
                        se.wait_ge(gate_full, b["gate_full"] + i + 1)
                        if st.what == "ple":
                            se.wait_ge(prod_done, b["prod_done"] + i)
                        elif not isinstance(i, int) or b["h_lo"] + i:
                            se.wait_ge(h_lo_done, b["h_lo"] + i)
                        gate = ps[:, 0:2, 0:HALF]
                        dst = act[:, :].rearrange("p (t n) -> p t n", t=2)
                        if st.what == "ffn":
                            se.activation(dst, gate, ACT.Silu).then_inc(act_done, 1)
                        else:
                            se.activation(dst, gate, ACT.Sigmoid,
                                          bias=gate_b[:, st.layer, bass.ds(i, 1)]).then_inc(act_done, 1)
                        next_cvt(st, i, 0, last)
                        if st.what == "ffn":
                            se.wait_ge(prod_done, b["prod_done"] + i + 1)
                            se.activation(h_hi[:, bass.ds(i, 1), :], act[:, :].rearrange("p (a n) -> p a n", a=1),
                                          ACT.Copy).then_inc(h_hi_done, 1)
                        se.wait_ge(up_full, b["up_full"] + i + 1)
                        next_cvt(st, i, 1, last)
                    if st.what == "ffn" and b["prod_done"]:
                        after(se, prod_done, b["prod_done"])
                    if st.what == "ple":
                        after(se, h_lo_done, b["h_lo"])
                        se.wait_ge(small_loaded, 32)
                    if not b["h_lo"]:
                        pair(0, False)
                    with se.Fori(0 if b["h_lo"] else 1, st.pairs - 1) as i:
                        pair(i, False)
                    pair(st.pairs - 1, True)
                elif st.kind == "tile":
                    def tiles(i, last):
                        for s in range(2):
                            se.wait_ge(acc_full, b["acc_full"] + 2 * i + s + 1)
                            if st.half == 0:
                                src = ps[:, 4 + 2 * s:6 + 2 * s, 0:HALF]
                                dst = y_t[:, bass.ds(2 * i + s, 1), :].rearrange("p a (t n) -> p (a t) n", t=2)
                                if st.what == "pool":
                                    se.activation(dst, src, ACT.Copy, scale=scale_p[:, bass.ds(2 * i + s, 1)]).then_inc(evac_act, 1)
                                else:
                                    se.activation(dst, src, ACT.Copy, scale=0.5 if st.what == "down" else 1.0).then_inc(evac_act, 1)
                            next_cvt(st, i, s, last)
                    if st.what == "pool":
                        se.wait_ge(small_loaded, 32)
                    with se.Fori(0, DC // 2 - 1) as i:
                        tiles(i, False)
                    tiles(DC // 2 - 1, True)
                elif st.kind == "attention":
                    def pair_of_heads(i, last):
                        def aux(m, dst, scale=1.0, cols=512, view=None):
                            se.wait_ge(aux_full[0], AUX * i + m + 1)
                            src = ps[:, 6, 0:cols]
                            se.activation(dst, view(src) if view else src, ACT.Copy, scale=scale).then_inc(aux_free[0], 1)

                        tiled = lambda v: v.rearrange("p (t n) -> p t n", n=P)
                        aux(0, q_t[:, 0:HALF], SCALE, HALF)
                        aux(1, v_t[:, 0:HALF], 1.0, HALF)
                        aux(2, k_t[:, 0:HALF], 1.0, HALF)
                        aux(3, v_tok[:, 0:4, :], view=tiled)
                        aux(4, k_tok[:, 0:4, :], view=tiled)

                        def keys(su):
                            for b2 in range(2):
                                aux(5 + 2 * su + b2, kc_t[:, b2, 0:4, :], view=tiled)

                        def weights(u):
                            se.wait_ge(s_full, NU * i + u + 1)
                            if u >= 2:
                                se.wait_ge(pv_done, NU * i + u - 1)
                            n = cols_of(u)
                            se.activation(wt[:, u % 2, 0:n], ps[:, u % 4, 0:n], ACT.Exp).then_inc(wt_done, 1)

                        for u in range(NU + 1):
                            if u < NU:
                                n = cols_of(u)
                                se.wait_ge(na_done, NU * i + u + 1)
                                se.activation(e_buf[:, u % 2, 0:n], e_buf[:, u % 2, 0:n], ACT.Exp).then_inc(el_done, 1)
                                se.wait_ge(el_done, 2 * (NU * i + u) + 1)
                                se.activation(e_buf[:, u % 2, 0:n], e_buf[:, u % 2, 0:n], ACT.Ln, bias=1.0).then_inc(el_done, 1)
                            if u + 1 in SAMPLE_AT:
                                keys(SAMPLE_AT.index(u + 1))
                            if u >= 1:
                                weights(u - 1)
                        se.wait_ge(pv_done, NU * i + NU)
                        se.activation(o_t[:, bass.ds(i, 1), 0:SEQ], ps[:, 4:5, :], ACT.Copy)
                        se.activation(o_t[:, bass.ds(i, 1), SEQ:], ps[:, 5:6, 0:P], ACT.Copy).then_inc(ot_act, 1)
                        for s in range(2):
                            next_cvt(st, i, s, last)
                        se.wait_ge(kv_stored, 64 * i + 64)
                    with se.Fori(0, PAIRS - 1) as i:
                        pair_of_heads(i, False)
                    pair_of_heads(PAIRS - 1, True)
                    se.wait_ge(ot_dve, PAIRS)
                    for c in range(DC):
                        se.activation(xt_hi[:, c, :], o_t[:, c, :], ACT.Copy).then_inc(x_hi_done, 1)

        @block.vector
        def _(ve):
            step = [0]

            def link(ins):
                step[0] += 1
                ins.then_inc(dve_step, 1)
                ve.wait_ge(dve_step, step[0])

            def cvt(n, s, k):
                ve.wait_ge(w_hi_done, n + 1)
                ve.tensor_tensor(w_lo[:, s, 0:k, :], w_raw[:, s, 0:k, :], w_hi[:, s, 0:k, :].bitcast(F32),
                                 ALU.subtract).then_inc(w_split, 1)

            def next_cvt(st, i, s, last):
                if not last:
                    cvt(st.base["w"] + 2 * i + s + 2, s, st.chunks[s])
                elif st.after is not None:
                    cvt(st.base["w"] + 2 * i + s + 2, s, st.after[s])

            first = next(s for s in stages if s.chunks[0])
            ve.wait_ge(const_step, 5)
            ve.tensor_copy(ident_r[:], ident[:])
            ve.tensor_copy(mask_r[:], mask_f[:]).then_inc(const_r, 1)

            for st in stages:
                b = st.base
                if st.kind == "norm":
                    def residual(t):
                        bank = 2 * (t % 2)
                        ve.wait_ge(yt_full, b["yt_full"] + t + 1)
                        ins = ve.scalar_tensor_tensor(x[:, t, :], x[:, t, :], ALPHA,
                                                      ps[:, bank:bank + 2, :].rearrange("p b n -> p (b n)"),
                                                      ALU.mult, ALU.add)
                        ins.then_inc(res_done, 1)
                        ve.wait_ge(res_done, b["res_done"] + t + 1)
                        ve.bn_stats(stats[:, t, 0:6], x[:, t, 0:512])
                        link(ve.bn_stats(stats[:, t, 6:12], x[:, t, 512:1024]))
                        ve.bn_aggr(mv[:, t, :], stats[:, t, :]).then_inc(stat_done, 1)

                    def normalise(t):
                        ve.wait_ge(std_done, b["std"] + t + 1)
                        ve.reciprocal(rstd[:, t:t + 1], std[:, t:t + 1])
                        if t == 0:
                            ve.wait_ge(gb_loaded, b["gb"] + 32)
                        link(ve.scalar_tensor_tensor(x[:, t, :], x[:, t, :], mv[:, t, 0:1], g_b[:, :],
                                                     ALU.subtract, ALU.mult))
                        ve.scalar_tensor_tensor(x[:, t, :], x[:, t, :], rstd[:, t:t + 1], b_b[:, :],
                                                ALU.mult, ALU.add).then_inc(x_norm, 1)

                    def low(t):
                        bank = 4 + 2 * (t % 2)
                        ve.wait_ge(x_hi_done, b["x_hi"] + t + 1)
                        cols = slice(t * P, (t + 1) * P)
                        ve.tensor_tensor(xt_lo[:, :, cols],
                                         ps[:, bank:bank + 2, :].rearrange("p b (c t) -> p (b c) t", t=P),
                                         xt_hi[:, :, cols].bitcast(F32), ALU.subtract).then_inc(x_lo_done, 1)

                    if st.what == "norm" and stages[stages.index(st) - 1].kind == "tile" and st.n == 1 and st.layer == 0:
                        ve.wait_ge(pool_stored, 16 * (1 + DEC_BATCH))
                    for t in range(TILES + 2):
                        if t < TILES and st.what == "norm":
                            residual(t)
                        if 1 <= t <= TILES and st.what == "norm":
                            normalise(t - 1)
                        if t >= 2 and st.then == "split":
                            low(t - 2)
                    if st is stages[0]:
                        cvt(0, 0, first.chunks[0])
                        cvt(1, 1, first.chunks[1])
                elif st.kind == "window":
                    after(ve, x_hi_done, b["x_hi"])
                    ve.wait_ge(state_done, 1)
                    ve.wait_ge(ext_zero, 1)

                    def window(c):
                        w = WINDOWS[c // 2]
                        if c:
                            ve.wait_ge(d_done, b["d_done"] + c)
                        src, reach = ext[:, c, :], 0
                        n = 0
                        while reach < w - 1:
                            hop = reach + 1
                            lo = reach + hop
                            link(ve.tensor_tensor(win[n % 2][:, lo:EXT], src[:, lo:EXT], src[:, lo - hop:EXT - hop], ALU.add))
                            src, reach, n = win[n % 2], lo, n + 1
                        head = src[:, PREV:PREV + w - 1]
                        link(ve.scalar_tensor_tensor(head, head, float(w), rcp[:, 0:w - 1], ALU.mult, ALU.mult))
                        ve.scalar_tensor_tensor(ext[:, c, PREV:], src[:, PREV:EXT], 1.0 / w, ext[:, c, PREV:],
                                                ALU.mult, ALU.subtract).then_inc(d_done, 1)

                    def low(c):
                        ve.wait_ge(d_hi_done, b["d_hi"] + c + 1)
                        ve.tensor_tensor(h_lo[:, c, 0:SEQ], ext[:, c, PREV:PREV + SEQ], h_hi[:, c, 0:SEQ].bitcast(F32),
                                         ALU.subtract)
                        own = ext[:, c, PREV + SEQ:].rearrange("p (b s) -> p b s", s=SEG)
                        ve.tensor_tensor(h_lo[:, c, SEQ:].rearrange("p (b s) -> p b s", s=DEC_SEQ), own[:, :, PREV:],
                                         h_hi[:, c, SEQ:].bitcast(F32).rearrange("p (b s) -> p b s", s=DEC_SEQ),
                                         ALU.subtract).then_inc(d_lo_done, 1)

                    for c in range(DC + 1):
                        if c < DC:
                            window(c)
                        if c >= 1:
                            low(c - 1)
                elif st.kind == "ple":
                    for c in range(PLE // P):
                        ve.wait_ge(pt_hi_done, b["pt_hi"] + c + 1)
                        ve.tensor_tensor(p_lo[:, c, :], ps[:, 4 + 2 * c:6 + 2 * c, :].rearrange("p b n -> p (b n)")[:, 0:TOKENS],
                                         p_hi[:, c, :].bitcast(F32), ALU.subtract).then_inc(pt_lo_done, 1)
                elif st.kind == "pair":
                    def pair(i, last):
                        next_cvt(st, i, 0, last)
                        ve.wait_ge(act_done, b["act_done"] + i + 1)
                        ve.wait_ge(up_full, b["up_full"] + i + 1)
                        gate = act[:, :].rearrange("p (t n) -> p t n", t=2)
                        up = ps[:, 2:4, 0:HALF]
                        if st.what == "ffn":
                            ve.tensor_tensor(gate, gate, up, ALU.mult).then_inc(prod_done, 1)
                            ve.wait_ge(h_hi_done, b["h_hi"] + i + 1)
                            ve.tensor_tensor(h_lo[:, bass.ds(i, 1), :], act[:, :].rearrange("p (a n) -> p a n", a=1),
                                             h_hi[:, bass.ds(i, 1), :].bitcast(F32), ALU.subtract).then_inc(h_lo_done, 1)
                        else:
                            ve.tensor_tensor(y_t[:, bass.ds(i, 1), :].rearrange("p a (t n) -> p (a t) n", t=2),
                                             gate, up, ALU.mult).then_inc(prod_done, 1)
                        next_cvt(st, i, 1, last)
                    with ve.Fori(0, st.pairs - 1) as i:
                        pair(i, False)
                    pair(st.pairs - 1, True)
                elif st.kind == "tile":
                    def tiles(i, last):
                        for s in range(2):
                            if st.half == 1:
                                ve.wait_ge(acc_full, b["acc_full"] + 2 * i + s + 1)
                                dst = y_t[:, bass.ds(2 * i + s, 1), :].rearrange("p a (t n) -> p (a t) n", t=2)
                                ve.scalar_tensor_tensor(dst, ps[:, 4 + 2 * s:6 + 2 * s, 0:HALF], 0.5, dst,
                                                        ALU.mult, ALU.add).then_inc(evac_dve, 1)
                            next_cvt(st, i, s, last)
                    if st.half == 1:
                        after(ve, evac_act, b["evac_act"])
                    with ve.Fori(0, DC // 2 - 1) as i:
                        tiles(i, False)
                    tiles(DC // 2 - 1, True)
                elif st.kind == "attention":
                    def pair_of_heads(i, last):
                        def aux(m, dst, scale=None, cols=512, view=None):
                            ve.wait_ge(aux_full[1], AUX * i + m + 1)
                            src = ps[:, 7, 0:cols]
                            src = view(src) if view else src
                            if scale:
                                ve.tensor_scalar(dst, src, scale, None, ALU.mult).then_inc(aux_free[1], 1)
                            else:
                                ve.tensor_copy(dst, src).then_inc(aux_free[1], 1)

                        tiled = lambda v: v.rearrange("p (t n) -> p t n", n=P)
                        aux(0, q_t[:, HALF:], SCALE, HALF)
                        ve.wait_ge(aux_free[1], AUX * i + 1)
                        for h in range(2):
                            rows = slice(HEAD_DIM * h, HEAD_DIM * (h + 1))
                            ve.tensor_copy(q_blk[rows, :, h, :],
                                           q_t[rows, SEQ:].rearrange("p (b s) -> p b s", s=DEC_SEQ)).then_inc(q_blk_done, 1)
                        aux(1, v_t[:, HALF:], None, HALF)
                        aux(2, k_t[:, HALF:], None, HALF)
                        aux(3, v_tok[:, 4, :], None, P)
                        aux(4, k_tok[:, 4, :], None, P)

                        def keys(su):
                            for b2 in range(2):
                                aux(5 + 2 * su + b2, kc_t[:, b2, 4:8, :], view=tiled)

                        def neg_abs(u):
                            n = cols_of(u)
                            ve.wait_ge(z_full, NU * i + u + 1)
                            ve.tensor_scalar(e_buf[:, u % 2, 0:n].bitcast(I32), ps[:, u % 4, 0:n].bitcast(I32), SIGN, None,
                                             ALU.bitwise_or).then_inc(na_done, 1)

                        def softplus(u):
                            n = cols_of(u)
                            ve.wait_ge(el_done, 2 * (NU * i + u) + 2)
                            if UNITS[u][0] == "p":
                                at = PART_AT[UNITS[u][2]]
                                dst = sp_p[:, UNITS[u][1], at:at + n]
                            else:
                                su = UNITS[u][1]
                                if su >= 2:
                                    ve.wait_ge(s_full, NU * i + SAMPLE_AT[su - 2] + 1)
                                dst = sp_s[:, su % 2].rearrange("p b k h s -> p (b k h s)")
                            ve.scalar_tensor_tensor(dst, ps[:, u % 4, 0:n], 0.0, e_buf[:, u % 2, 0:n],
                                                    ALU.max, ALU.add).then_inc(sp_done, 1)

                        neg_abs(0)
                        for u in range(NU):
                            if u + 1 in SAMPLE_AT:
                                keys(SAMPLE_AT.index(u + 1))
                            if u + 1 < NU:
                                neg_abs(u + 1)
                            softplus(u)
                        ve.wait_ge(ot_act, i + 1)
                        for h in range(2):
                            rows = slice(HEAD_DIM * h, HEAD_DIM * (h + 1))
                            dst = o_t[rows, bass.ds(i, 1), SEQ:].rearrange("p a (b s) -> p (a b) s", s=DEC_SEQ)
                            past = ps[rows, 5, P:P + 2 * P].rearrange("p (b h s) -> p b h s", h=2, s=DEC_SEQ)[:, :, h, :]
                            ins = ve.tensor_tensor(dst, dst, past, ALU.add)
                        ins.then_inc(ot_dve, 1)
                        for s in range(2):
                            next_cvt(st, i, s, last)
                        ve.wait_ge(kv_stored, 64 * i + 64)
                    ve.wait_ge(q_blk_zero, 1)
                    with ve.Fori(0, PAIRS - 1) as i:
                        pair_of_heads(i, False)
                    pair_of_heads(PAIRS - 1, True)
                    for c in range(DC):
                        ve.wait_ge(x_hi_done, b["x_hi"] + c + 1)
                        ve.tensor_tensor(xt_lo[:, c, :], o_t[:, c, :], xt_hi[:, c, :].bitcast(F32),
                                         ALU.subtract).then_inc(x_lo_done, 1)

        @block.tensor
        def _(pe):
            def products(s, chunks, x_hi, x_lo, bank, first=True, last=True, only=(0, 1)):
                n = len(chunks)
                for j, (cw, cx) in enumerate(chunks):
                    for w, xx in ((w_hi, x_hi), (w_hi, x_lo), (w_lo, x_hi)):
                        for half in only:
                            ins = pe.matmul(ps[:, bank[half], 0:HALF], w[:, s, cw, :],
                                            xx(cx, half), start=(first and j == 0 and w is w_hi and xx is x_hi),
                                            stop=(last and j == n - 1 and w is w_lo), skip_group_check=True)
                return ins

            def moving(t):
                return lambda c, half: t[:, c, half * HALF:(half + 1) * HALF]

            same = lambda n: [(c, c) for c in range(n)]
            pe.wait_ge(const_step, 5)
            pe.wait_ge(const_r, 1)

            for st in stages:
                b = st.base
                if st.kind == "norm":
                    if st.what == "norm":
                        after(pe, evac_act, b["evac_act"])
                        after(pe, evac_dve, b["evac_dve"])
                        after(pe, prod_done, b["prod_done"])
                    for t in range(TILES + 1):
                        if t < TILES and st.what == "norm":
                            if t >= 2:
                                pe.wait_ge(res_done, b["res_done"] + t - 1)
                            bank = 2 * (t % 2)
                            for c in range(DC):
                                ins = pe.transpose(ps[:, bank + c // 4, (c % 4) * P:(c % 4 + 1) * P],
                                                   y_t[:, c, t * P:(t + 1) * P], ident[:])
                            ins.then_inc(yt_full, 1)
                        if t >= 1 and st.then != "none":
                            n = t - 1
                            if st.what == "norm":
                                pe.wait_ge(x_norm, b["x_norm"] + n + 1)
                            elif n == 0:
                                pe.wait_ge(x_loaded, 16 * TILES)
                            if n >= 2:
                                if st.then == "split":
                                    pe.wait_ge(x_lo_done, b["x_lo"] + n - 1)
                                else:
                                    pe.wait_ge(x_hi_done, b["x_hi"] + n - 1)
                            bank = 4 + 2 * (n % 2)
                            for c in range(DC):
                                ins = pe.transpose(ps[:, bank + c // 4, (c % 4) * P:(c % 4 + 1) * P],
                                                   x[:, n, c * P:(c + 1) * P], ident[:])
                            ins.then_inc(xt_full, 1)
                elif st.kind == "window":
                    pe.wait_ge(state_loaded, 16)
                    after(pe, res_done, b["res_done"])
                    rows = DEC_BATCH * PREV
                    for c in range(DC):
                        ins = pe.transpose(ps[:, c // 4, (c % 4) * P:(c % 4) * P + rows],
                                           state_t[:, c * P:(c + 1) * P], ident[0:rows, 0:rows])
                    ins.then_inc(state_full, 1)
                elif st.kind == "ple":
                    pe.wait_ge(p_loaded, 32 * (st.layer + 1))
                    after(pe, x_lo_done, b["x_lo"])
                    for c in range(PLE // P):
                        for t in range(TILES):
                            ins = pe.transpose(ps[:, 4 + 2 * c + t // 4, (t % 4) * P:(t % 4 + 1) * P],
                                               p_tok[:, t, c * P:(c + 1) * P], ident[:])
                        ins.then_inc(pt_full, 1)
                elif st.kind == "pair":
                    after(pe, x_lo_done, b["x_lo"])
                    if st.what == "ple":
                        after(pe, pt_lo_done, b["pt_lo"])

                    def pair(i, begun):
                        pe.wait_ge(w_split, b["w"] + 2 * i + 1)
                        if begun:
                            pe.wait_ge(act_done, b["act_done"] + i)
                        products(0, same(DC), moving(xt_hi), moving(xt_lo), (0, 1)).then_inc(gate_full, 1)
                        pe.wait_ge(w_split, b["w"] + 2 * i + 2)
                        if begun:
                            pe.wait_ge(prod_done, b["prod_done"] + i)
                        own = (xt_hi, xt_lo) if st.what == "ffn" else (p_hi, p_lo)
                        products(1, same(st.chunks[1]), moving(own[0]), moving(own[1]), (2, 3)).then_inc(up_full, 1)

                    if not b["act_done"]:
                        pair(0, False)
                    with pe.Fori(0 if b["act_done"] else 1, st.pairs) as i:
                        pair(i, True)
                elif st.kind == "tile":
                    if st.what == "out":
                        after(pe, x_lo_done, b["x_lo"])
                    after(pe, evac_act, b["evac_act"])
                    after(pe, evac_dve, b["evac_dve"])
                    free = evac_dve if st.half else evac_act
                    base = b["evac_dve"] if st.half else b["evac_act"]
                    if st.what == "down":
                        after(pe, h_lo_done, b["h_lo"])

                    def tiles(i, begun):
                        for s in range(2):
                            if begun:
                                pe.wait_ge(free, base + 2 * i + s - 1)
                            pe.wait_ge(w_split, b["w"] + 2 * i + s + 1)
                            bank = (4 + 2 * s, 5 + 2 * s)
                            if st.what == "down":
                                ins = products(s, same(FH), moving(h_hi), moving(h_lo), bank)
                            elif st.what == "out":
                                ins = products(s, same(DC), moving(xt_hi), moving(xt_lo), bank)
                            else:
                                pe.wait_ge(d_lo_done, b["d_lo"] - DC + 2 * i + 2)
                                def of(t):
                                    return lambda c, half: t[:, bass.ds(2 * i + c, 1), half * HALF:(half + 1) * HALF]
                                ins = products(s, same(2), of(h_hi), of(h_lo), bank)
                            ins.then_inc(acc_full, 1)
                    tiles(0, False)
                    with pe.Fori(1, DC // 2) as i:
                        tiles(i, True)
                elif st.kind == "attention":
                    after(pe, x_lo_done, b["x_lo"])
                    after(pe, evac_dve, b["evac_dve"])
                    attend(pe, st, products, moving)

_INS = ["x_prompt", "x_sample", "cache_k", "cache_v", "state_pool", "p_prompt", "p_sample", "ln_g", "ln_b", "ffn_w1",
        "ffn_w3", "ffn_w2", "pool_w", "pool_scale", "sb_w_in", "sb_w_out", "ple_w_gate", "ple_b_gate", "ple_w_proj"]
_OUTS = [(1, SEQ, D_MODEL), (DEC_BATCH, DEC_SEQ, D_MODEL), (1, 1, SEQ, HEADS, HEAD_DIM), (1, 1, SEQ, HEADS, HEAD_DIM),
         (1, DEC_BATCH, DEC_SEQ, HEADS, HEAD_DIM), (1, DEC_BATCH, DEC_SEQ, HEADS, HEAD_DIM), (1, 1, PREV, D_MODEL),
         (1, DEC_BATCH, PREV, D_MODEL)]


def kernel(**inputs):
    import numpy as _np
    import concourse.bacc as _bacc
    from concourse import mybir as _mybir
    from concourse.bass_utils import run_bass_kernel_spmd as _run

    nc = _bacc.Bacc("TRN2", target_bir_lowering=False, num_devices=1)
    arrays, args = {}, []
    for name in _INS:
        a = _np.ascontiguousarray(inputs[name])
        arrays[f"in_{name}_dram"] = a
        args.append(nc.dram_tensor(f"in_{name}_dram", a.shape, _mybir.dt.from_np(a.dtype), kind="ExternalInput").ap())
    for n, shape in enumerate(_OUTS):
        args.append(nc.dram_tensor(f"out_{n}_dram", shape, _mybir.dt.float32, kind="ExternalOutput").ap())
    streaming_trunk(nc, *args)
    r = _run(nc, [arrays], core_ids=[0])
    return tuple(r.results[0][f"out_{n}_dram"] for n in range(len(_OUTS)))
```

```python
from contextlib import ExitStack

import concourse.bass as bass
from concourse import mybir

P = 128
D_MODEL = 1024
SEQ = 512
DEPTH = 2
DEC_BATCH = 8
DEC_SEQ = 16
PAST = 1024
HEADS = 16
HEAD_DIM = D_MODEL // HEADS
WINDOWS = (2, 4, 8, 16)
PREV = max(WINDOWS) - 1
D_FF = 2816
PLE = 256
ALPHA = (2.0 * DEPTH) ** 0.25
EPS = 1e-5
SCALE = HEAD_DIM ** -0.5
MASKED = -(2.0 ** 99)

TOKENS = SEQ + DEC_BATCH * DEC_SEQ
TILES = TOKENS // P
PROMPT_TILES = SEQ // P
HALF = TOKENS // 2
DC = D_MODEL // P
FC = D_FF // P
FH = FC // 2
PAIRS = HEADS // 2
SLOT = 12
EXT = PREV + SEQ + DEC_BATCH * (PREV + DEC_SEQ)
SEG = PREV + DEC_SEQ
KEY_BLOCKS = PAST // P

F32 = mybir.dt.float32
F32R = mybir.dt.float32r
I32 = mybir.dt.int32
SIGN = -(1 << 31)
ALU = mybir.AluOpType
ACT = mybir.ActivationFunctionType

UNITS = [("p", 0, 0), ("p", 1, 0), ("p", 0, 1), ("s", 0), ("p", 1, 1), ("s", 1), ("p", 0, 2), ("s", 2), ("p", 1, 2),
         ("s", 3)]
NU = len(UNITS)
SAMPLE_AT = [u for u, unit in enumerate(UNITS) if unit[0] == "s"]
PART_AT = (0, 512, 896)
PART_COLS = (512, 384, 512)
SB = 4
AUX = (13, 14)
TOTALS_USE = 7


def keys_uses(which, su):
    return 5 + 2 * (su + 1) + (1 if which == 1 and su else 0)


class Stage:

    def __init__(self, kind, chunks=(0, 0), what="", layer=0, n=0, half=0, pairs=0, then=""):
        self.kind, self.chunks, self.what, self.layer = kind, chunks, what, layer
        self.n, self.half, self.pairs, self.then = n, half, pairs, then
        self.base = {}
        self.landed = 0
        self.after = None


def plan_stages():
    stages = []

    def add(kind, chunks=(0, 0), **more):
        stages.append(Stage(kind, chunks, **more))

    def ffn(layer, n):
        for half in range(2):
            add("pair", (DC, DC), pairs=FH, what="ffn", layer=layer, n=n, half=half)
            add("tile", (FH, FH), what="down", layer=layer, n=n, half=half)

    add("norm", what="load", then="split", layer=0, n=0)
    for layer in range(DEPTH):
        pool = layer % 2 == 0
        last = layer == DEPTH - 1
        ffn(layer, 0)
        add("norm", what="norm", layer=layer, n=0, then="window" if pool else "split")
        if pool:
            add("window", layer=layer)
            add("tile", (2, 2), what="pool", layer=layer, half=0)
        else:
            add("attention", (SLOT, SLOT), layer=layer)
            add("tile", (DC, DC), what="out", layer=layer, half=0)
        add("norm", what="norm", layer=layer, n=1, then="split")
        ffn(layer, 1)
        add("norm", what="norm", layer=layer, n=2, then="split")
        add("ple", layer=layer)
        add("pair", (DC, PLE // P), pairs=DC, what="ple", layer=layer)
        add("norm", what="norm", layer=layer, n=3, then="none" if last else "split")

    value = {}
    for st in stages:
        st.base = {k: value.get(k, 0) for k in NAMES}
        for k, v in increments(st).items():
            value[k] = value.get(k, 0) + v
    for st, nxt in zip(stages, stages[1:] + [None]):
        after = [s for s in stages[stages.index(st) + 1:] if s.chunks[0]]
        st.after = after[0].chunks if after else None
    return stages


def after(engine, semaphore, value):
    if value:
        engine.wait_ge(semaphore, value)


NAMES = ["w", "gate_full", "up_full", "act_done", "prod_done", "h_hi", "h_lo", "acc_full", "evac_act", "evac_dve",
         "yt_full", "res_done", "stat", "std", "x_norm", "xt_full", "x_hi", "x_lo", "gb", "d_done", "d_hi", "d_lo",
         "pt_full", "pt_hi", "pt_lo", "state"]


def increments(st):
    if st.kind == "pair":
        n = dict.fromkeys(["gate_full", "up_full", "act_done", "prod_done"], st.pairs)
        if st.what == "ffn":
            n.update(h_hi=st.pairs, h_lo=st.pairs)
        return n | {"w": 2 * st.pairs}
    if st.kind == "tile":
        return {"w": DC, "acc_full": DC, ("evac_dve" if st.half else "evac_act"): DC}
    if st.kind == "norm":
        n = {}
        if st.what == "norm":
            n = dict.fromkeys(["yt_full", "res_done", "stat", "std", "x_norm"], TILES) | {"gb": 32}
        if st.then != "none":
            n.update(xt_full=TILES, x_hi=TILES)
        if st.then == "split":
            n.update(x_lo=TILES)
        return n
    if st.kind == "window":
        return {"d_done": DC, "d_hi": DC, "d_lo": DC, "state": 16}
    if st.kind == "ple":
        return {"pt_full": 2, "pt_hi": 2, "pt_lo": 2}
    if st.kind == "attention":
        return {"w": 2 * PAIRS, "x_hi": DC, "x_lo": DC}
    raise ValueError(st.kind)


def streaming_trunk(nc, x_prompt, x_sample, cache_k, cache_v, state_pool, p_prompt, p_sample, ln_g, ln_b, ffn_w1,
                    ffn_w3, ffn_w2, pool_w, pool_scale, sb_w_in, sb_w_out, ple_w_gate, ple_b_gate, ple_w_proj,
                    y_prompt, y_sample, new_k_prompt, new_v_prompt, new_k_sample, new_v_sample, new_pool_prompt,
                    new_pool_sample):
    stages = plan_stages()
    attention = next(s for s in stages if s.kind == "attention")
    norms = [s for s in stages if s.kind == "norm" and s.what == "norm"]

    with ExitStack() as ctx:
        def sb(name, shape, dt=F32):
            return ctx.enter_context(nc.sbuf_tensor(name, shape, dt))

        def sem(name):
            return ctx.enter_context(nc.semaphore(name))

        x = sb("x", [P, TILES, D_MODEL])
        y_t = sb("y_t", [P, DC, TOKENS])
        w_raw = sb("w_raw", [P, 2, SLOT, P])
        w_hi = sb("w_hi", [P, 2, SLOT, P], F32R)
        w_lo = sb("w_lo", [P, 2, SLOT, P], F32R)
        act = sb("act", [P, TOKENS])
        ident = sb("ident", [P, P])
        ident_r = sb("ident_r", [P, P], F32R)
        neg_tri = sb("neg_tri", [P, P])
        neg_ones = sb("neg_ones", [P, P])
        mask_f = sb("mask_f", [P, 2, P])
        mask_r = sb("mask_r", [P, 2, P], F32R)
        rcp = sb("rcp", [P, PREV])
        eps = sb("eps", [P, 1])
        one = sb("one", [P, 1])
        stats = sb("stats", [P, TILES, 12])
        mv = sb("mv", [P, TILES, 2])
        std = sb("std", [P, TILES])
        rstd = sb("rstd", [P, TILES])
        gate_b = sb("gate_b", [P, DEPTH, DC])
        scale_p = sb("scale_p", [P, DC])

        at_xt = ctx.enter_context(nc.sbuf_tensor("region_xt", [P, 2 * DC * TOKENS], F32))
        at_gb = ctx.enter_context(nc.sbuf_tensor("region_gb", [P, 2 * D_MODEL], F32))
        arena_bytes = 76320
        at_arena = ctx.enter_context(nc.sbuf_tensor("region_arena", [P, arena_bytes // 4], F32))
        sizes = {at_xt.name: 8 * DC * TOKENS, at_gb.name: 8 * D_MODEL, at_arena.name: arena_bytes}
        used = {}

        def place(where, name, shape, dt=F32, at=None):
            nbytes = 4
            for n in shape[1:]:
                nbytes *= n
            start = used.get(where.name, 0) if at is None else at
            used[where.name] = start + nbytes
            assert used[where.name] <= sizes[where.name], (name, used[where.name], sizes[where.name])
            base = nc.lookup_mls(where.name).memorylocations[0].addr
            return nc.alloc_sbuf_tensor_at(name, shape, dt, offset=base + start)

        xt_hi = place(at_xt, "xt_hi", [P, DC, TOKENS], F32R)
        xt_lo = place(at_xt, "xt_lo", [P, DC, TOKENS], F32R)
        ext = place(at_xt, "ext", [P, DC, EXT], at=0)
        state_t = place(at_xt, "state_t", [DEC_BATCH * PREV, D_MODEL])
        win = [place(at_xt, f"win{n}", [P, EXT + 1]) for n in range(2)]

        g_b = place(at_gb, "g_b", [P, D_MODEL])
        b_b = place(at_gb, "b_b", [P, D_MODEL])
        q_t = place(at_gb, "q_t", [P, TOKENS], at=0)
        k_t = place(at_gb, "k_t", [P, TOKENS])
        k_tok = place(at_gb, "k_tok", [P, TILES, P])

        h_hi = place(at_arena, "h_hi", [P, FH, TOKENS], F32R)
        h_lo = place(at_arena, "h_lo", [P, FH, TOKENS], F32R)
        p_tok = place(at_arena, "p_tok", [P, TILES, PLE])
        p_hi = place(at_arena, "p_hi", [P, PLE // P, TOKENS], F32R)
        p_lo = place(at_arena, "p_lo", [P, PLE // P, TOKENS], F32R)
        k_raw = place(at_arena, "k_raw", [P, 2, SB, SB, P], at=0)
        v_raw = place(at_arena, "v_raw", [P, 2, SB, SB, P])
        kc_t = place(at_arena, "kc_t", [P, SB, SB, P])
        sp_p = place(at_arena, "sp_p", [P, 2, sum(PART_COLS)])
        relu_s = place(at_arena, "relu_s", [P, 2, 512])
        s_sum = place(at_arena, "s_sum", [P, 2, 512])
        total = place(at_arena, "total", [P, 8])
        e_buf = place(at_arena, "e_buf", [P, 2, 512])
        wt = place(at_arena, "wt", [P, 3, 512])
        q_blk = place(at_arena, "q_blk", [P, DEC_BATCH, 2, DEC_SEQ])
        v_tok = place(at_arena, "v_tok", [P, TILES, P])
        own_sp = place(at_arena, "own_sp", [P, DEC_BATCH, 2, DEC_SEQ])
        o_past = place(at_arena, "o_past", [P, 2, P])
        v_t = act
        o_t = y_t
        ps = ctx.enter_context(nc.psum_tensor("ps", [P, 8, 512], F32))

        const_step = sem("const_step")
        const_r = sem("const_r")
        x_loaded = sem("x_loaded")
        small_loaded = sem("small_loaded")
        w_loaded = [sem("w_loaded0"), sem("w_loaded1")]
        w_hi_done = sem("w_hi_done")
        w_split = sem("w_split")
        gate_full = sem("gate_full")
        up_full = sem("up_full")
        act_done = sem("act_done")
        prod_done = sem("prod_done")
        h_hi_done = sem("h_hi_done")
        h_lo_done = sem("h_lo_done")
        acc_full = sem("acc_full")
        evac_act = sem("evac_act")
        evac_dve = sem("evac_dve")
        yt_full = sem("yt_full")
        res_done = sem("res_done")
        stat_done = sem("stat_done")
        std_done = sem("std_done")
        x_norm = sem("x_norm")
        xt_full = sem("xt_full")
        x_hi_done = sem("x_hi_done")
        x_lo_done = sem("x_lo_done")
        gb_loaded = sem("gb_loaded")
        dve_step = sem("dve_step")
        state_loaded = sem("state_loaded")
        state_full = sem("state_full")
        state_done = sem("state_done")
        ext_zero = sem("ext_zero")
        d_done = sem("d_done")
        d_hi_done = sem("d_hi_done")
        d_lo_done = sem("d_lo_done")
        p_loaded = sem("p_loaded")
        pt_full = sem("pt_full")
        pt_hi_done = sem("pt_hi_done")
        pt_lo_done = sem("pt_lo_done")
        k_loaded = [sem("k_loaded0"), sem("k_loaded1")]
        v_loaded = [sem("v_loaded0"), sem("v_loaded1")]
        aux_full = [sem("aux_full_a"), sem("aux_full_v")]
        aux_free = [sem("aux_free_a"), sem("aux_free_v")]
        q_blk_zero = sem("q_blk_zero")
        q_blk_done = sem("q_blk_done")
        z_full = sem("z_full")
        na_done = sem("na_done")
        el_done = sem("el_done")
        sp_done = sem("sp_done")
        own_copied = sem("own_copied")
        relu_done = sem("relu_done")
        arg_done = sem("arg_done")
        w_rows_done = sem("w_rows_done")
        past_saved = sem("past_saved")
        past_full = sem("past_full")
        s_full = sem("s_full")
        wt_done = sem("wt_done")
        pv_done = sem("pv_done")
        ot_act = sem("ot_act")
        ot_dve = sem("ot_dve")
        kv_stored = sem("kv_stored")
        pool_stored = sem("pool_stored")
        y_stored = sem("y_stored")

        xp = x_prompt[0].rearrange("(t p) d -> p t d", p=P)
        xs = x_sample.rearrange("b s d -> (b s) d")

        def block_source(st, s, i):
            if st.kind == "pair" and st.what == "ffn":
                w = (ffn_w1, ffn_w3)[s][st.layer, st.n].rearrange("(c p) f -> p c f", p=P)
                return [(0, DC, w[:, :, bass.ds(i * P + st.half * FH * P, P)])]
            if st.kind == "pair":
                w = (ple_w_gate, ple_w_proj)[s][st.layer].rearrange("(c p) f -> p c f", p=P)
                return [(0, st.chunks[s], w[:, :, bass.ds(i * P, P)])]
            if st.kind == "tile" and st.what == "down":
                w = ffn_w2[st.layer, st.n].rearrange("(c p) f -> p c f", p=P)
                return [(0, FH, w[:, st.half * FH:(st.half + 1) * FH, bass.ds(i * 2 * P + s * P, P)])]
            if st.kind == "tile" and st.what == "out":
                w = sb_w_out[0].rearrange("(c p) f -> p c f", p=P)
                return [(0, DC, w[:, :, bass.ds(i * 2 * P + s * P, P)])]
            if st.kind == "tile":
                w = pool_w[0].rearrange("g (c p) f -> p g c f", p=P)
                return [(0, 2, w[:, i, :, s * P:(s + 1) * P])]
            w = sb_w_in[0].rearrange("(c p) (m f) -> p c m f", p=P, m=3)
            col = bass.ds(i * P, P)
            if s == 0:
                return [(0, DC, w[:, :, 0, col]), (DC, 4, w[:, 0:4, 2, col])]
            return [(0, 4, w[:, 4:8, 2, col]), (4, DC, w[:, :, 1, col])]

        def block_loads(st):
            return 32 if st.kind == "attention" else 16

        def iterations(st):
            return st.pairs if st.kind == "pair" else PAIRS if st.kind == "attention" else DC // 2

        landed = 0
        for st in stages:
            if st.chunks[0]:
                st.landed = landed
                landed += block_loads(st) * iterations(st)

        def after_stage(st):
            later = [s for s in stages[stages.index(st) + 1:] if s.chunks[0]]
            return later[0] if later else None

        kc = cache_k[0].rearrange("b (k p) h d -> p b k (h d)", p=P)
        vc = cache_v[0].rearrange("b (k p) h d -> p b k (h d)", p=P)

        def attend_pool(pool, st):
            after(pool, evac_dve, st.base["evac_dve"])
            pool.memset(q_blk[:], 0.0).then_inc(q_blk_zero, 1)
            k_out = new_k_prompt[0, 0].rearrange("(t p) h d -> p t (h d)", p=P)
            v_out = new_v_prompt[0, 0].rearrange("(t p) h d -> p t (h d)", p=P)
            ks_out = new_k_sample[0].rearrange("b s h d -> (b s) (h d)")
            vs_out = new_v_sample[0].rearrange("b s h d -> (b s) (h d)")
            with pool.Fori(0, PAIRS) as i:
                col = bass.ds(i * P, P)
                pool.wait_ge(aux_free[0], AUX[0] * i + 5)
                pool.wait_ge(aux_free[1], AUX[1] * i + 5)
                pool.dma_start(k_out[:, :, col], k_tok[:, 0:PROMPT_TILES, :]).then_inc(kv_stored, 16)
                pool.dma_start(ks_out[:, col], k_tok[:, PROMPT_TILES, :]).then_inc(kv_stored, 16)
                pool.dma_start(v_out[:, :, col], v_tok[:, 0:PROMPT_TILES, :]).then_inc(kv_stored, 16)
                pool.dma_start(vs_out[:, col], v_tok[:, PROMPT_TILES, :]).then_inc(kv_stored, 16)

        def cols_of(u):
            return PART_COLS[UNITS[u][2]] if UNITS[u][0] == "p" else 512

        def attend(pe, st, products, moving):
            b = st.base

            def mm(out, w, xx, start=False):
                return pe.matmul(out, w, xx, start=start, stop=True, skip_group_check=True)

            uses = [0, 0]

            def aux_wait(i, which):
                if not isinstance(i, int) or AUX[which] * i + uses[which]:
                    pe.wait_ge(aux_free[which], AUX[which] * i + uses[which])
                uses[which] += 1

            def project(i, parts):
                aux_wait(i, 0)
                aux_wait(i, 1)
                for n, (s, chunks) in enumerate(parts):
                    for half in range(2):
                        ins = products(s, chunks, moving(xt_hi), moving(xt_lo), (6, 7), first=(n == 0),
                                       last=(n == len(parts) - 1), only=(half,))
                        if n == len(parts) - 1:
                            ins.then_inc(aux_full[half], 1)

            def project_q(i):
                uses[:] = [0, 0]
                pe.wait_ge(w_split, b["w"] + 2 * i + 1)
                project(i, [(0, [(c, c) for c in range(8)])])

            def project_v(i):
                pe.wait_ge(w_split, b["w"] + 2 * i + 2)
                project(i, [(0, [(8 + c, c) for c in range(4)]), (1, [(c, 4 + c) for c in range(4)])])

            def project_k(i):
                project(i, [(1, [(4 + c, c) for c in range(8)])])

            def to_tokens(i, src, evacuated):
                for which in range(2):
                    pe.wait_ge(aux_free[which], AUX[which] * i + evacuated)
                aux_wait(i, 0)
                for t in range(PROMPT_TILES):
                    ins = pe.transpose(ps[:, 6, t * P:(t + 1) * P], src[:, t * P:(t + 1) * P], ident[:])
                ins.then_inc(aux_full[0], 1)
                aux_wait(i, 1)
                pe.transpose(ps[:, 7, 0:P], src[:, SEQ:], ident[:]).then_inc(aux_full[1], 1)

            def pair_of_heads(i, begun, last):
                def cached_keys(su):
                    slot = su % 2
                    pe.wait_ge(k_loaded[slot], 128 * i + 64 * (su // 2) + 64)
                    for j in range(SB):
                        which = j % 2
                        aux_wait(i, which)
                        for kb in range(SB):
                            ins = pe.transpose(ps[:, 6 + which, kb * P:(kb + 1) * P], k_raw[:, slot, j, kb, :], ident[:])
                        ins.then_inc(aux_full[which], 1)

                def own_totals():
                    pe.wait_ge(own_copied, 2 * i + 2)
                    aux_wait(i, 1)
                    for b8 in range(DEC_BATCH):
                        g, j = divmod(b8, SB)
                        ins = mm(ps[32 * j:32 * (j + 1), 7, g:g + 1],
                                 own_sp[:, b8].rearrange("p h s -> p (h s)"), one[:, 0:1], start=True)
                    ins.then_inc(aux_full[1], 1)

                def scores(u):
                    if u >= 4:
                        pe.wait_ge(wt_done, NU * i + u - 3)
                    z = ps[:, u % 4, :]
                    if UNITS[u][0] == "p":
                        _, h, part = UNITS[u]
                        rows = slice(HEAD_DIM * h, HEAD_DIM * (h + 1))
                        blocks = {0: [(3, 0, 0), (2, P, 0), (4, 3 * P, 1)], 1: [(1, 0, 0)], 2: [(0, 0, 0)]}[part]
                        first = True
                        for kb, at, mask in blocks:
                            stop = TOKENS if kb == 4 else SEQ
                            n = stop - kb * P
                            mm(z[:, at:at + n], k_t[rows, kb * P:(kb + 1) * P], q_t[rows, kb * P:stop], start=first)
                            ins = mm(z[:, at:at + P], ident_r[:], mask_r[:, mask, :])
                            first = False
                    else:
                        su = UNITS[u][1]
                        pe.wait_ge(q_blk_done, 2 * i + 2)
                        for which in range(2):
                            pe.wait_ge(aux_free[which], AUX[which] * i + keys_uses(which, su))
                        for j in range(SB):
                            ins = mm(ps[32 * j:32 * (j + 1), u % 4, :],
                                     q_blk[:, SB * (su // 2) + j].rearrange("p h s -> p (h s)"),
                                     kc_t[:, j].rearrange("p k n -> p (k n)"), start=True)
                    ins.then_inc(z_full, 1)

                def suffix(u):
                    z = ps[:, u % 4, :]
                    if UNITS[u][0] == "p":
                        pe.wait_ge(sp_done, NU * i + u + 1)
                        _, h, part = UNITS[u]
                        sp = sp_p[:, h, :]
                        at, n = PART_AT[part], PART_COLS[part]
                        ins = mm(z[:, 0:n], neg_tri[:], sp[:, at:at + n])
                        kb3, kb2, kb1 = sp[:, 0:P], sp[:, P:3 * P], sp[:, 512:896]
                        later = {0: [(2 * P, 3 * P, kb3)], 1: [(P, 3 * P, kb2), (2 * P, 3 * P, kb3)],
                                 2: [(P, 4 * P, kb1), (2 * P, 4 * P, kb2), (3 * P, 4 * P, kb3)]}[part]
                        for lo, hi, src in later:
                            ins = mm(z[:, lo:hi], neg_ones[:], src)
                    else:
                        su = UNITS[u][1]
                        pe.wait_ge(w_rows_done, 4 * i + su + 1)
                        for kb in range(SB):
                            ins = pe.transpose(z[:, kb * P:(kb + 1) * P], relu_s[:, su % 2, kb * P:(kb + 1) * P], ident[:])
                    ins.then_inc(s_full, 1)

                def values(u):
                    pe.wait_ge(wt_done, NU * i + u + 1)
                    if u == 0:
                        for which in range(2):
                            pe.wait_ge(aux_free[which], AUX[which] * i + 4)
                        if begun:
                            pe.wait_ge(ot_dve, i)
                    w = wt[:, u % 3, :]
                    if UNITS[u][0] == "p":
                        _, h, part = UNITS[u]
                        rows = slice(HEAD_DIM * h, HEAD_DIM * (h + 1))
                        v = lambda kb: v_tok[:, kb, rows]
                        if part == 0:
                            mm(ps[rows, 4, 3 * P:4 * P], v(3), w[:, 0:P], start=True)
                            mm(ps[rows, 4, 2 * P:4 * P], v(2), w[:, P:3 * P])
                            ins = mm(ps[rows, 5, 0:P], v(4), w[:, 3 * P:4 * P], start=True)
                        elif part == 1:
                            ins = mm(ps[rows, 4, P:4 * P], v(1), w[:, 0:3 * P])
                        else:
                            ins = mm(ps[rows, 4, :], v(0), w)
                    else:
                        su = UNITS[u][1]
                        slot = su % 2
                        pe.wait_ge(v_loaded[slot], 128 * i + 64 * (su // 2) + 64)
                        at = (1 + su // 2) * P
                        for kb in range(SB):
                            for j in range(SB):
                                ins = mm(ps[32 * j:32 * (j + 1), 5, at:at + P], w[:, kb * P + 32 * j:kb * P + 32 * (j + 1)],
                                         v_raw[:, slot, j, kb, :])
                    ins.then_inc(pv_done, 1)

                fill = {NU - 1: project_q, NU + 1: project_v, NU + 3: project_k}
                for u in range(NU + 4):
                    if u < NU:
                        if u == 0:
                            for which in range(2):
                                pe.wait_ge(aux_free[which], AUX[which] * i + 3)
                        scores(u)
                    if u + 1 in SAMPLE_AT:
                        cached_keys(SAMPLE_AT.index(u + 1))
                    if u == 3:
                        own_totals()
                    if 2 <= u < NU + 2:
                        suffix(u - 2)
                    if u >= 4:
                        values(u - 4)
                    if u in fill and not last:
                        fill[u](i + 1)
                pe.wait_ge(past_saved, i + 1)
                for g in range(2):
                    ins = pe.transpose(ps[:, 5, (1 + g) * P:(2 + g) * P], o_past[:, g, :], ident[:])
                ins.then_inc(past_full, 1)
                if not last:
                    to_tokens(i + 1, v_t, 2)
                    to_tokens(i + 1, k_t, 3)

            project_q(0)
            project_v(0)
            project_k(0)
            to_tokens(0, v_t, 2)
            to_tokens(0, k_t, 3)
            pair_of_heads(0, False, False)
            with pe.Fori(1, PAIRS - 1) as i:
                pair_of_heads(i, True, False)
            pair_of_heads(PAIRS - 1, True, True)


        block = ctx.enter_context(nc.Block())

        @block.sync
        def _(sp):
            for t in range(PROMPT_TILES):
                sp.dma_start(x[:, t, :], xp[:, t, :]).then_inc(x_loaded, 16)
            sp.dma_start(x[:, PROMPT_TILES, :], xs).then_inc(x_loaded, 16)

            def load_blocks(st, i, wait=True):
                for s in range(2):
                    if wait:
                        sp.wait_ge(w_split, st.base["w"] + 2 * i + s - 1)
                    for c0, n, src in block_source(st, s, i):
                        sp.dma_start(w_raw[:, s, c0:c0 + n, :], src).then_inc(w_loaded[s], 16)

            def load_cache(i, su):
                col = bass.ds(i * P, P)
                slot = su % 2
                blocks = slice(SB, 2 * SB) if su % 2 == 0 else slice(0, SB)
                if su >= 2:
                    sp.wait_ge(aux_full[1], AUX[1] * i + keys_uses(1, su - 2))
                elif not isinstance(i, int) or i:
                    sp.wait_ge(aux_full[1], AUX[1] * i - AUX[1] + keys_uses(1, su + 2))
                for j in reversed(range(SB)):
                    sp.dma_start(k_raw[:, slot, j], kc[:, SB * (su // 2) + j, blocks, col]).then_inc(k_loaded[slot], 16)
                if su >= 2:
                    sp.wait_ge(pv_done, NU * i + SAMPLE_AT[su - 2] + 1)
                elif not isinstance(i, int) or i:
                    sp.wait_ge(pv_done, NU * i - NU + SAMPLE_AT[su + 2] + 1)
                for j in range(SB):
                    sp.dma_start(v_raw[:, slot, j], vc[:, SB * (su // 2) + j, blocks, col]).then_inc(v_loaded[slot], 16)

            for st in stages:
                if not st.chunks[0]:
                    continue
                if st.kind != "attention":
                    if st.base["w"] == 0:
                        load_blocks(st, 0, wait=False)
                    with sp.Fori(1 if st.base["w"] == 0 else 0, iterations(st)) as i:
                        load_blocks(st, i)
                    continue
                load_blocks(st, 0)
                load_blocks(st, 1)
                after(sp, evac_dve, st.base["evac_dve"])
                for su in range(4):
                    load_cache(0, su)
                with sp.Fori(1, PAIRS - 1) as i:
                    load_blocks(st, i + 1)
                    for su in range(4):
                        load_cache(i, su)
                for su in range(4):
                    load_cache(PAIRS - 1, su)

        @block.gpsimd
        def _(pool):
            step = [0]

            def link(ins):
                step[0] += 1
                ins.then_inc(const_step, 1)
                pool.wait_ge(const_step, step[0])

            pool.dma_start(gate_b[:, :, :], ple_b_gate.rearrange("l (c p) -> p l c", p=P),
                           allow_slow_non_contiguous=True).then_inc(small_loaded, 16)
            pool.dma_start(scale_p[:, :], pool_scale[0].rearrange("(c p) -> p c", p=P),
                           allow_slow_non_contiguous=True).then_inc(small_loaded, 16)

            def load_gb(st):
                for dst, src in ((g_b, ln_g), (b_b, ln_b)):
                    row = src[st.layer, st.n:st.n + 1, :]
                    pool.dma_start(dst[:, :], row.broadcast_to([P, D_MODEL])).then_inc(gb_loaded, 16)

            def load_p(layer):
                pool.dma_start(p_tok[:, 0:PROMPT_TILES, :],
                               p_prompt[layer, 0].rearrange("(t p) d -> p t d", p=P)).then_inc(p_loaded, 16)
                pool.dma_start(p_tok[:, PROMPT_TILES, :],
                               p_sample[layer].rearrange("b s d -> (b s) d")).then_inc(p_loaded, 16)

            load_gb(norms[0])
            load_p(0)
            pool.memset(ident[:], 0.0)
            pool.memset(neg_tri[:], -1.0)
            pool.memset(neg_ones[:], -1.0)
            pool.memset(eps[:], EPS)
            pool.memset(one[:], 1.0)
            for t in range(PREV):
                pool.memset(rcp[:, t:t + 1], 1.0 / (t + 1))
            link(pool.memset(mask_f[:], 0.0))
            link(pool.affine_select(out=ident[:], in_=ident[:], compare_op=ALU.not_equal, fill=1.0, base=0,
                                    pattern=[[-1, P]], channel_multiplier=1))
            link(pool.affine_select(out=neg_tri[:], in_=neg_tri[:], compare_op=ALU.is_ge, fill=0.0, base=0,
                                    pattern=[[-1, P]], channel_multiplier=1))
            link(pool.affine_select(out=mask_f[:], in_=mask_f[:], compare_op=ALU.is_gt, fill=MASKED, base=0,
                                    pattern=[[0, 2], [1, P]], channel_multiplier=-1))
            own = mask_f[:, 1, :].rearrange("p (b s) -> p b s", s=DEC_SEQ)
            link(pool.affine_select(out=own, in_=own, compare_op=ALU.is_ge, fill=MASKED, base=0,
                                    pattern=[[-DEC_SEQ, DEC_BATCH], [0, DEC_SEQ]], channel_multiplier=1))

            norm_index = 0
            for st in stages:
                b = st.base
                if st.kind == "norm" and st.what == "norm":
                    norm_index += 1
                    pool.wait_ge(x_norm, b["x_norm"] + TILES)
                    if norm_index < len(norms) and norms[norm_index].base["w"] <= attention.base["w"]:
                        load_gb(norms[norm_index])
                    elif norm_index < len(norms) and st.base["w"] > attention.base["w"]:
                        load_gb(norms[norm_index])
                    if st.then == "window":
                        pool.dma_start(new_pool_prompt[0, 0], x[P - PREV:P, PROMPT_TILES - 1, :]).then_inc(pool_stored, 16)
                        for n in range(DEC_BATCH):
                            lo = (n + 1) * DEC_SEQ - PREV
                            pool.dma_start(new_pool_sample[0, n], x[lo:lo + PREV, PROMPT_TILES, :]).then_inc(pool_stored, 16)
                    if st.then == "none":
                        pool.dma_start(y_prompt[0].rearrange("(t p) d -> p t d", p=P),
                                       x[:, 0:PROMPT_TILES, :]).then_inc(y_stored, 16)
                        pool.dma_start(y_sample.rearrange("b s d -> (b s) d"),
                                       x[:, PROMPT_TILES, :]).then_inc(y_stored, 16)
                if st.kind == "tile" and st.what == "down" and st.half == 1 and st.layer == 0 and st.n == 0:
                    after(pool, up_full, b["up_full"])
                    pool.dma_start(state_t[:, :], state_pool[0].rearrange("b r d -> (b r) d")).then_inc(state_loaded, 16)
                    pool.memset(ext[:, :, 0:PREV], 0.0).then_inc(ext_zero, 1)
                if st.kind == "attention":
                    attend_pool(pool, st)
                    pool.wait_ge(kv_stored, 64 * PAIRS)
                    pool.wait_ge(ot_dve, PAIRS)
                    load_gb(norms[norm_index])
                    load_p(1)
            pool.wait_ge(pool_stored, 16 * (1 + DEC_BATCH))
            pool.wait_ge(kv_stored, 64 * PAIRS)
            pool.wait_ge(y_stored, 32)

        @block.scalar
        def _(se):
            def cvt(st, n, s, landed_at):
                k = st.chunks[s]
                se.wait_ge(w_loaded[s], landed_at)
                se.activation(w_hi[:, s, 0:k, :], w_raw[:, s, 0:k, :], ACT.Copy).then_inc(w_hi_done, 1)

            def cvt_of(st, i, s):
                cvt(st, None, s, st.landed + block_loads(st) * (i + 1))

            def next_cvt(st, i, s, last):
                if not last:
                    cvt_of(st, i + 1, s)
                elif after_stage(st) is not None:
                    cvt_of(after_stage(st), 0, s)

            first = next(s for s in stages if s.chunks[0])

            for st in stages:
                b = st.base
                if st.kind == "norm":
                    for t in range(TILES + 1):
                        if t < TILES and st.what == "norm":
                            se.wait_ge(stat_done, b["stat"] + t + 1)
                            se.activation(std[:, t:t + 1], mv[:, t, 1:2], ACT.Sqrt, bias=eps[:, 0:1]).then_inc(std_done, 1)
                        if t >= 1 and st.then != "none":
                            n = t - 1
                            bank = 4 + 2 * (n % 2)
                            se.wait_ge(xt_full, b["xt_full"] + n + 1)
                            tile = ps[:, bank:bank + 2, :].rearrange("p b n -> p (b n)")
                            if st.then == "split":
                                se.activation(xt_hi[:, :, n * P:(n + 1) * P],
                                              tile.rearrange("p (c t) -> p c t", t=P), ACT.Copy).then_inc(x_hi_done, 1)
                            elif n < PROMPT_TILES:
                                se.activation(ext[:, :, PREV + n * P:PREV + (n + 1) * P],
                                              tile.rearrange("p (c t) -> p c t", t=P), ACT.Copy).then_inc(x_hi_done, 1)
                            else:
                                for q in range(2):
                                    cc = slice(4 * q, 4 * q + 4)
                                    own = ext[:, cc, PREV + SEQ:].rearrange("p c (b s) -> p c b s", s=SEG)
                                    ins = se.activation(own[:, :, :, PREV:],
                                                        ps[:, bank + q, :].rearrange("p (c b s) -> p c b s", c=4, s=DEC_SEQ),
                                                        ACT.Copy)
                                ins.then_inc(x_hi_done, 1)
                    if st is stages[0]:
                        cvt_of(first, 0, 0)
                        cvt_of(first, 0, 1)
                elif st.kind == "window":
                    se.wait_ge(state_full, 1)
                    for q in range(2):
                        own = ext[:, 4 * q:4 * q + 4, PREV + SEQ:].rearrange("p c (b s) -> p c b s", s=SEG)
                        src = ps[:, q, :].rearrange("p (c r) -> p c r", c=4)[:, :, 0:DEC_BATCH * PREV]
                        ins = se.activation(own[:, :, :, 0:PREV], src.rearrange("p c (b s) -> p c b s", s=PREV), ACT.Copy)
                    ins.then_inc(state_done, 1)
                    for c in range(DC):
                        se.wait_ge(d_done, b["d_done"] + c + 1)
                        se.activation(h_hi[:, c, 0:SEQ], ext[:, c, PREV:PREV + SEQ], ACT.Copy)
                        own = ext[:, c, PREV + SEQ:].rearrange("p (b s) -> p b s", s=SEG)
                        se.activation(h_hi[:, c, SEQ:].rearrange("p (b s) -> p b s", s=DEC_SEQ), own[:, :, PREV:],
                                      ACT.Copy).then_inc(d_hi_done, 1)
                elif st.kind == "ple":
                    for c in range(PLE // P):
                        se.wait_ge(pt_full, b["pt_full"] + c + 1)
                        se.activation(p_hi[:, c, :], ps[:, 4 + 2 * c:6 + 2 * c, :].rearrange("p b n -> p (b n)")[:, 0:TOKENS],
                                      ACT.Copy).then_inc(pt_hi_done, 1)
                elif st.kind == "pair":
                    def pair(i, last):
                        se.wait_ge(gate_full, b["gate_full"] + i + 1)
                        if st.what == "ple":
                            se.wait_ge(prod_done, b["prod_done"] + i)
                        elif not isinstance(i, int) or b["h_lo"] + i:
                            se.wait_ge(h_lo_done, b["h_lo"] + i)
                        gate = ps[:, 0:2, 0:HALF]
                        dst = act[:, :].rearrange("p (t n) -> p t n", t=2)
                        if st.what == "ffn":
                            se.activation(dst, gate, ACT.Silu).then_inc(act_done, 1)
                        else:
                            se.activation(dst, gate, ACT.Sigmoid,
                                          bias=gate_b[:, st.layer, bass.ds(i, 1)]).then_inc(act_done, 1)
                        next_cvt(st, i, 0, last)
                        if st.what == "ffn":
                            se.wait_ge(prod_done, b["prod_done"] + i + 1)
                            se.activation(h_hi[:, bass.ds(i, 1), :], act[:, :].rearrange("p (a n) -> p a n", a=1),
                                          ACT.Copy).then_inc(h_hi_done, 1)
                        se.wait_ge(up_full, b["up_full"] + i + 1)
                        next_cvt(st, i, 1, last)
                    if st.what == "ffn" and b["prod_done"]:
                        after(se, prod_done, b["prod_done"])
                    if st.what == "ple":
                        after(se, h_lo_done, b["h_lo"])
                        se.wait_ge(small_loaded, 32)
                    if st.what == "ffn":
                        se.preload_act_table(ACT.Silu)
                    else:
                        se.preload_act_table(ACT.Sigmoid)
                    if not b["h_lo"]:
                        pair(0, False)
                    with se.Fori(0 if b["h_lo"] else 1, st.pairs - 1) as i:
                        pair(i, False)
                    pair(st.pairs - 1, True)
                elif st.kind == "tile":
                    def tiles(i, last):
                        for s in range(2):
                            se.wait_ge(acc_full, b["acc_full"] + 2 * i + s + 1)
                            if st.half == 0:
                                src = ps[:, 4 + 2 * s:6 + 2 * s, 0:HALF]
                                dst = y_t[:, bass.ds(2 * i + s, 1), :].rearrange("p a (t n) -> p (a t) n", t=2)
                                if st.what == "pool":
                                    se.activation(dst, src, ACT.Copy, scale=scale_p[:, bass.ds(2 * i + s, 1)]).then_inc(evac_act, 1)
                                else:
                                    se.activation(dst, src, ACT.Copy, scale=0.5 if st.what == "down" else 1.0).then_inc(evac_act, 1)
                            next_cvt(st, i, s, last)
                    if st.what == "pool":
                        se.wait_ge(small_loaded, 32)
                    with se.Fori(0, DC // 2 - 1) as i:
                        tiles(i, False)
                    tiles(DC // 2 - 1, True)
                elif st.kind == "attention":
                    def aux(i, m, dst, scale=1.0, cols=512, tiled=False):
                        se.wait_ge(aux_full[0], AUX[0] * i + m + 1)
                        src = ps[:, 6, 0:cols]
                        if tiled:
                            src = src.rearrange("p (t n) -> p t n", n=P)
                        se.activation(dst, src, ACT.Copy, scale=scale).then_inc(aux_free[0], 1)

                    def weights(i, u):
                        se.wait_ge(s_full, NU * i + u + 1)
                        if u >= 3:
                            se.wait_ge(pv_done, NU * i + u - 2)
                        n = cols_of(u)
                        func = ACT.Exp if UNITS[u][0] == "p" else ACT.Copy
                        se.activation(wt[:, u % 3, 0:n], ps[:, u % 4, 0:n], func).then_inc(wt_done, 1)

                    def pair_of_heads(i, last):
                        for u in range(NU + 2):
                            if u < NU:
                                n = cols_of(u)
                                e = e_buf[:, u % 2, 0:n]
                                se.wait_ge(na_done, NU * i + u + 1)
                                se.activation(e, e, ACT.Exp).then_inc(el_done, 1)
                                se.wait_ge(el_done, 2 * (NU * i + u) + 1)
                                se.activation(e, e, ACT.Ln, bias=1.0).then_inc(el_done, 1)
                            if u + 1 in SAMPLE_AT:
                                su = SAMPLE_AT.index(u + 1)
                                for j in (0, 2):
                                    aux(i, 5 + 2 * su + j // 2, kc_t[:, j], tiled=True)
                            if u - 1 in SAMPLE_AT:
                                su = SAMPLE_AT.index(u - 1)
                                se.wait_ge(arg_done, 4 * i + su + 1)
                                se.activation(relu_s[:, su % 2, :], relu_s[:, su % 2, :], ACT.Exp).then_inc(w_rows_done, 1)
                            if u >= 2:
                                weights(i, u - 2)
                            if u in (2, 4) and not last:
                                next_cvt(st, i, u // 2 - 1, last)
                            if u == NU - 1 and not last:
                                aux(i + 1, 0, q_t[:, 0:HALF], SCALE, HALF)
                        if not last:
                            aux(i + 1, 1, v_t[:, 0:HALF], 1.0, HALF)
                        se.wait_ge(pv_done, NU * i + NU)
                        se.activation(o_t[:, bass.ds(i, 1), 0:SEQ], ps[:, 4:5, :], ACT.Copy)
                        se.activation(o_t[:, bass.ds(i, 1), SEQ:], ps[:, 5:6, 0:P], ACT.Copy).then_inc(ot_act, 1)
                        se.activation(o_past[:, :, :], ps[:, 5, P:3 * P].rearrange("p (g n) -> p g n", g=2),
                                      ACT.Copy).then_inc(past_saved, 1)
                        if not last:
                            aux(i + 1, 2, k_t[:, 0:HALF], 1.0, HALF)
                        se.wait_ge(kv_stored, 64 * i + 64)
                        if not last:
                            aux(i + 1, 3, v_tok[:, 0:4, :], tiled=True)
                            aux(i + 1, 4, k_tok[:, 0:4, :], tiled=True)

                    se.preload_act_table_set("natural_log_exp_and_others")
                    aux(0, 0, q_t[:, 0:HALF], SCALE, HALF)
                    aux(0, 1, v_t[:, 0:HALF], 1.0, HALF)
                    aux(0, 2, k_t[:, 0:HALF], 1.0, HALF)
                    aux(0, 3, v_tok[:, 0:4, :], tiled=True)
                    aux(0, 4, k_tok[:, 0:4, :], tiled=True)
                    with se.Fori(0, PAIRS - 1) as i:
                        pair_of_heads(i, False)
                    pair_of_heads(PAIRS - 1, True)
                    se.wait_ge(ot_dve, PAIRS)
                    for c in range(DC):
                        se.activation(xt_hi[:, c, :], o_t[:, c, :], ACT.Copy).then_inc(x_hi_done, 1)
                    for s in range(2):
                        next_cvt(st, PAIRS - 1, s, True)

        @block.vector
        def _(ve):
            step = [0]

            def link(ins):
                step[0] += 1
                ins.then_inc(dve_step, 1)
                ve.wait_ge(dve_step, step[0])

            def cvt(n, s, k):
                ve.wait_ge(w_hi_done, n + 1)
                ve.tensor_tensor(w_lo[:, s, 0:k, :], w_raw[:, s, 0:k, :], w_hi[:, s, 0:k, :].bitcast(F32),
                                 ALU.subtract).then_inc(w_split, 1)

            def next_cvt(st, i, s, last):
                if not last:
                    cvt(st.base["w"] + 2 * i + s + 2, s, st.chunks[s])
                elif st.after is not None:
                    cvt(st.base["w"] + 2 * i + s + 2, s, st.after[s])

            first = next(s for s in stages if s.chunks[0])
            ve.wait_ge(const_step, 5)
            ve.tensor_copy(ident_r[:], ident[:])
            ve.tensor_copy(mask_r[:], mask_f[:]).then_inc(const_r, 1)

            for st in stages:
                b = st.base
                if st.kind == "norm":
                    def residual(t):
                        bank = 2 * (t % 2)
                        ve.wait_ge(yt_full, b["yt_full"] + t + 1)
                        ins = ve.scalar_tensor_tensor(x[:, t, :], x[:, t, :], ALPHA,
                                                      ps[:, bank:bank + 2, :].rearrange("p b n -> p (b n)"),
                                                      ALU.mult, ALU.add)
                        ins.then_inc(res_done, 1)
                        ve.wait_ge(res_done, b["res_done"] + t + 1)
                        ve.bn_stats(stats[:, t, 0:6], x[:, t, 0:512])
                        link(ve.bn_stats(stats[:, t, 6:12], x[:, t, 512:1024]))
                        ve.bn_aggr(mv[:, t, :], stats[:, t, :]).then_inc(stat_done, 1)

                    def normalise(t):
                        ve.wait_ge(std_done, b["std"] + t + 1)
                        ve.reciprocal(rstd[:, t:t + 1], std[:, t:t + 1])
                        if t == 0:
                            ve.wait_ge(gb_loaded, b["gb"] + 32)
                        link(ve.scalar_tensor_tensor(x[:, t, :], x[:, t, :], mv[:, t, 0:1], g_b[:, :],
                                                     ALU.subtract, ALU.mult))
                        ve.scalar_tensor_tensor(x[:, t, :], x[:, t, :], rstd[:, t:t + 1], b_b[:, :],
                                                ALU.mult, ALU.add).then_inc(x_norm, 1)

                    def low(t):
                        bank = 4 + 2 * (t % 2)
                        ve.wait_ge(x_hi_done, b["x_hi"] + t + 1)
                        cols = slice(t * P, (t + 1) * P)
                        ve.tensor_tensor(xt_lo[:, :, cols],
                                         ps[:, bank:bank + 2, :].rearrange("p b (c t) -> p (b c) t", t=P),
                                         xt_hi[:, :, cols].bitcast(F32), ALU.subtract).then_inc(x_lo_done, 1)

                    if st.what == "norm" and stages[stages.index(st) - 1].kind == "tile" and st.n == 1 and st.layer == 0:
                        ve.wait_ge(pool_stored, 16 * (1 + DEC_BATCH))
                    for t in range(TILES + 2):
                        if t < TILES and st.what == "norm":
                            residual(t)
                        if 1 <= t <= TILES and st.what == "norm":
                            normalise(t - 1)
                        if t >= 2 and st.then == "split":
                            low(t - 2)
                    if st is stages[0]:
                        cvt(0, 0, first.chunks[0])
                        cvt(1, 1, first.chunks[1])
                elif st.kind == "window":
                    after(ve, x_hi_done, b["x_hi"])
                    ve.wait_ge(state_done, 1)
                    ve.wait_ge(ext_zero, 1)

                    def window(c):
                        w = WINDOWS[c // 2]
                        if c:
                            ve.wait_ge(d_done, b["d_done"] + c)
                        src, reach = ext[:, c, :], 0
                        n = 0
                        while reach < w - 1:
                            hop = reach + 1
                            lo = reach + hop
                            link(ve.tensor_tensor(win[n % 2][:, lo:EXT], src[:, lo:EXT], src[:, lo - hop:EXT - hop], ALU.add))
                            src, reach, n = win[n % 2], lo, n + 1
                        head = src[:, PREV:PREV + w - 1]
                        link(ve.scalar_tensor_tensor(head, head, float(w), rcp[:, 0:w - 1], ALU.mult, ALU.mult))
                        ve.scalar_tensor_tensor(ext[:, c, PREV:], src[:, PREV:EXT], 1.0 / w, ext[:, c, PREV:],
                                                ALU.mult, ALU.subtract).then_inc(d_done, 1)

                    def low(c):
                        ve.wait_ge(d_hi_done, b["d_hi"] + c + 1)
                        ve.tensor_tensor(h_lo[:, c, 0:SEQ], ext[:, c, PREV:PREV + SEQ], h_hi[:, c, 0:SEQ].bitcast(F32),
                                         ALU.subtract)
                        own = ext[:, c, PREV + SEQ:].rearrange("p (b s) -> p b s", s=SEG)
                        ve.tensor_tensor(h_lo[:, c, SEQ:].rearrange("p (b s) -> p b s", s=DEC_SEQ), own[:, :, PREV:],
                                         h_hi[:, c, SEQ:].bitcast(F32).rearrange("p (b s) -> p b s", s=DEC_SEQ),
                                         ALU.subtract).then_inc(d_lo_done, 1)

                    for c in range(DC + 1):
                        if c < DC:
                            window(c)
                        if c >= 1:
                            low(c - 1)
                elif st.kind == "ple":
                    for c in range(PLE // P):
                        ve.wait_ge(pt_hi_done, b["pt_hi"] + c + 1)
                        ve.tensor_tensor(p_lo[:, c, :], ps[:, 4 + 2 * c:6 + 2 * c, :].rearrange("p b n -> p (b n)")[:, 0:TOKENS],
                                         p_hi[:, c, :].bitcast(F32), ALU.subtract).then_inc(pt_lo_done, 1)
                elif st.kind == "pair":
                    def pair(i, last):
                        next_cvt(st, i, 0, last)
                        ve.wait_ge(act_done, b["act_done"] + i + 1)
                        ve.wait_ge(up_full, b["up_full"] + i + 1)
                        gate = act[:, :].rearrange("p (t n) -> p t n", t=2)
                        up = ps[:, 2:4, 0:HALF]
                        if st.what == "ffn":
                            ve.tensor_tensor(gate, gate, up, ALU.mult).then_inc(prod_done, 1)
                            ve.wait_ge(h_hi_done, b["h_hi"] + i + 1)
                            ve.tensor_tensor(h_lo[:, bass.ds(i, 1), :], act[:, :].rearrange("p (a n) -> p a n", a=1),
                                             h_hi[:, bass.ds(i, 1), :].bitcast(F32), ALU.subtract).then_inc(h_lo_done, 1)
                        else:
                            ve.tensor_tensor(y_t[:, bass.ds(i, 1), :].rearrange("p a (t n) -> p (a t) n", t=2),
                                             gate, up, ALU.mult).then_inc(prod_done, 1)
                        next_cvt(st, i, 1, last)
                    with ve.Fori(0, st.pairs - 1) as i:
                        pair(i, False)
                    pair(st.pairs - 1, True)
                elif st.kind == "tile":
                    def tiles(i, last):
                        for s in range(2):
                            if st.half == 1:
                                ve.wait_ge(acc_full, b["acc_full"] + 2 * i + s + 1)
                                dst = y_t[:, bass.ds(2 * i + s, 1), :].rearrange("p a (t n) -> p (a t) n", t=2)
                                ve.scalar_tensor_tensor(dst, ps[:, 4 + 2 * s:6 + 2 * s, 0:HALF], 0.5, dst,
                                                        ALU.mult, ALU.add).then_inc(evac_dve, 1)
                            next_cvt(st, i, s, last)
                    if st.half == 1:
                        after(ve, evac_act, b["evac_act"])
                    with ve.Fori(0, DC // 2 - 1) as i:
                        tiles(i, False)
                    tiles(DC // 2 - 1, True)
                elif st.kind == "attention":
                    def aux(i, m, dst, scale=None, cols=512, tiled=False):
                        ve.wait_ge(aux_full[1], AUX[1] * i + m + 1)
                        src = ps[:, 7, 0:cols]
                        if tiled:
                            src = src.rearrange("p (t n) -> p t n", n=P)
                        if scale:
                            ve.tensor_scalar(dst, src, scale, None, ALU.mult).then_inc(aux_free[1], 1)
                        else:
                            ve.tensor_copy(dst, src).then_inc(aux_free[1], 1)

                    def evac_q(i):
                        aux(i, 0, q_t[:, HALF:], SCALE, HALF)
                        ve.wait_ge(aux_free[1], AUX[1] * i + 1)
                        for h in range(2):
                            rows = slice(HEAD_DIM * h, HEAD_DIM * (h + 1))
                            ve.tensor_copy(q_blk[rows, :, h, :],
                                           q_t[rows, SEQ:].rearrange("p (b s) -> p b s", s=DEC_SEQ)).then_inc(q_blk_done, 1)

                    def evac_tokens(i):
                        aux(i, 3, v_tok[:, 4, :], None, P)
                        aux(i, 4, k_tok[:, 4, :], None, P)

                    def pair_of_heads(i, last):
                        def neg_abs(u):
                            n = cols_of(u)
                            ve.wait_ge(z_full, NU * i + u + 1)
                            if u >= 2:
                                ve.wait_ge(sp_done, NU * i + u - 1)
                            ve.tensor_scalar(e_buf[:, u % 2, 0:n].bitcast(I32), ps[:, u % 4, 0:n].bitcast(I32), SIGN, None,
                                             ALU.bitwise_or).then_inc(na_done, 1)
                            if UNITS[u][0] == "s":
                                su = UNITS[u][1]
                                if su >= 2:
                                    ve.wait_ge(s_full, NU * i + SAMPLE_AT[su - 2] + 1)
                                ve.tensor_scalar(relu_s[:, su % 2, :], ps[:, u % 4, :], 0.0, None,
                                                 ALU.max).then_inc(relu_done, 1)

                        def softplus(u):
                            n = cols_of(u)
                            ve.wait_ge(el_done, 2 * (NU * i + u) + 2)
                            at = PART_AT[UNITS[u][2]]
                            dst = sp_p[:, UNITS[u][1], at:at + n]
                            ve.scalar_tensor_tensor(dst, ps[:, u % 4, 0:n], 0.0, e_buf[:, u % 2, 0:n],
                                                    ALU.max, ALU.add).then_inc(sp_done, 1)
                            if u == 1:
                                ve.wait_ge(sp_done, NU * i + 2)
                                for h in range(2):
                                    ve.tensor_copy(own_sp[:, :, h, :],
                                                   sp_p[:, h, 3 * P:4 * P].rearrange("p (b s) -> p b s", s=DEC_SEQ)
                                                   ).then_inc(own_copied, 1)

                        def suffix(u):
                            su = UNITS[u][1]
                            slot = su % 2
                            ve.wait_ge(el_done, 2 * (NU * i + u) + 2)
                            ve.wait_ge(relu_done, 4 * i + su + 1)
                            if su == 0:
                                ve.wait_ge(aux_free[1], AUX[1] * i + TOTALS_USE + 1)
                            else:
                                ve.wait_ge(arg_done, 4 * i + su)
                            start = s_sum[:, 0, 0:1] if slot else total[:, su // 2:su // 2 + 1]
                            ve.tensor_tensor_scan(s_sum[:, slot, ::-1], e_buf[:, u % 2, ::-1], relu_s[:, slot, ::-1], start,
                                                  ALU.add, ALU.add).then_inc(sp_done, 1)
                            ve.wait_ge(sp_done, NU * i + u + 1)
                            ve.tensor_tensor(relu_s[:, slot, :], ps[:, u % 4, :], s_sum[:, slot, :],
                                             ALU.subtract).then_inc(arg_done, 1)

                        neg_abs(0)
                        for u in range(NU):
                            if u + 1 in SAMPLE_AT:
                                su = SAMPLE_AT.index(u + 1)
                                for j in (1, 3):
                                    aux(i, keys_uses(1, su) - 2 + j // 2, kc_t[:, j], tiled=True)
                            if u == 3:
                                aux(i, TOTALS_USE, total[:, 0:2], None, 2)
                            if u + 1 < NU:
                                neg_abs(u + 1)
                            if UNITS[u][0] == "p":
                                softplus(u)
                            else:
                                suffix(u)
                            if u in (2, 4) and not last:
                                next_cvt(st, i, u // 2 - 1, last)
                        if not last:
                            evac_q(i + 1)
                            aux(i + 1, 1, v_t[:, HALF:], None, HALF)
                            aux(i + 1, 2, k_t[:, HALF:], None, HALF)
                        ve.wait_ge(ot_act, i + 1)
                        ve.wait_ge(past_full, i + 1)
                        for h in range(2):
                            rows = slice(HEAD_DIM * h, HEAD_DIM * (h + 1))
                            dst = o_t[rows, bass.ds(i, 1), SEQ:].rearrange("p a (b s) -> p (a b) s", s=DEC_SEQ)
                            past = ps[rows, 5, P:P + 2 * P].rearrange("p (b h s) -> p b h s", h=2, s=DEC_SEQ)[:, :, h, :]
                            ins = ve.tensor_tensor(dst, dst, past, ALU.add)
                        ins.then_inc(ot_dve, 1)
                        ve.wait_ge(kv_stored, 64 * i + 64)
                        if not last:
                            evac_tokens(i + 1)

                    ve.wait_ge(q_blk_zero, 1)
                    evac_q(0)
                    aux(0, 1, v_t[:, HALF:], None, HALF)
                    aux(0, 2, k_t[:, HALF:], None, HALF)
                    evac_tokens(0)
                    with ve.Fori(0, PAIRS - 1) as i:
                        pair_of_heads(i, False)
                    pair_of_heads(PAIRS - 1, True)
                    for c in range(DC):
                        ve.wait_ge(x_hi_done, b["x_hi"] + c + 1)
                        ve.tensor_tensor(xt_lo[:, c, :], o_t[:, c, :], xt_hi[:, c, :].bitcast(F32),
                                         ALU.subtract).then_inc(x_lo_done, 1)
                    for s in range(2):
                        next_cvt(st, PAIRS - 1, s, True)

        @block.tensor
        def _(pe):
            def products(s, chunks, x_hi, x_lo, bank, first=True, last=True, only=(0, 1)):
                n = len(chunks)
                for j, (cw, cx) in enumerate(chunks):
                    for w, xx in ((w_hi, x_hi), (w_hi, x_lo), (w_lo, x_hi)):
                        for half in only:
                            ins = pe.matmul(ps[:, bank[half], 0:HALF], w[:, s, cw, :],
                                            xx(cx, half), start=(first and j == 0 and w is w_hi and xx is x_hi),
                                            stop=(last and j == n - 1 and w is w_lo), skip_group_check=True)
                return ins

            def moving(t):
                return lambda c, half: t[:, c, half * HALF:(half + 1) * HALF]

            same = lambda n: [(c, c) for c in range(n)]
            pe.wait_ge(const_step, 5)
            pe.wait_ge(const_r, 1)

            for st in stages:
                b = st.base
                if st.kind == "norm":
                    if st.what == "norm":
                        after(pe, evac_act, b["evac_act"])
                        after(pe, evac_dve, b["evac_dve"])
                        after(pe, prod_done, b["prod_done"])
                    for t in range(TILES + 1):
                        if t < TILES and st.what == "norm":
                            if t >= 2:
                                pe.wait_ge(res_done, b["res_done"] + t - 1)
                            bank = 2 * (t % 2)
                            for c in range(DC):
                                ins = pe.transpose(ps[:, bank + c // 4, (c % 4) * P:(c % 4 + 1) * P],
                                                   y_t[:, c, t * P:(t + 1) * P], ident[:])
                            ins.then_inc(yt_full, 1)
                        if t >= 1 and st.then != "none":
                            n = t - 1
                            if st.what == "norm":
                                pe.wait_ge(x_norm, b["x_norm"] + n + 1)
                            elif n == 0:
                                pe.wait_ge(x_loaded, 16 * TILES)
                            if n >= 2:
                                if st.then == "split":
                                    pe.wait_ge(x_lo_done, b["x_lo"] + n - 1)
                                else:
                                    pe.wait_ge(x_hi_done, b["x_hi"] + n - 1)
                            bank = 4 + 2 * (n % 2)
                            for c in range(DC):
                                ins = pe.transpose(ps[:, bank + c // 4, (c % 4) * P:(c % 4 + 1) * P],
                                                   x[:, n, c * P:(c + 1) * P], ident[:])
                            ins.then_inc(xt_full, 1)
                elif st.kind == "window":
                    pe.wait_ge(state_loaded, 16)
                    after(pe, res_done, b["res_done"])
                    rows = DEC_BATCH * PREV
                    for c in range(DC):
                        ins = pe.transpose(ps[:, c // 4, (c % 4) * P:(c % 4) * P + rows],
                                           state_t[:, c * P:(c + 1) * P], ident[0:rows, 0:rows])
                    ins.then_inc(state_full, 1)
                elif st.kind == "ple":
                    pe.wait_ge(p_loaded, 32 * (st.layer + 1))
                    after(pe, x_lo_done, b["x_lo"])
                    for c in range(PLE // P):
                        for t in range(TILES):
                            ins = pe.transpose(ps[:, 4 + 2 * c + t // 4, (t % 4) * P:(t % 4 + 1) * P],
                                               p_tok[:, t, c * P:(c + 1) * P], ident[:])
                        ins.then_inc(pt_full, 1)
                elif st.kind == "pair":
                    after(pe, x_lo_done, b["x_lo"])
                    if st.what == "ple":
                        after(pe, pt_lo_done, b["pt_lo"])

                    def pair(i, begun):
                        pe.wait_ge(w_split, b["w"] + 2 * i + 1)
                        if begun:
                            pe.wait_ge(act_done, b["act_done"] + i)
                        products(0, same(DC), moving(xt_hi), moving(xt_lo), (0, 1)).then_inc(gate_full, 1)
                        pe.wait_ge(w_split, b["w"] + 2 * i + 2)
                        if begun:
                            pe.wait_ge(prod_done, b["prod_done"] + i)
                        own = (xt_hi, xt_lo) if st.what == "ffn" else (p_hi, p_lo)
                        products(1, same(st.chunks[1]), moving(own[0]), moving(own[1]), (2, 3)).then_inc(up_full, 1)

                    if not b["act_done"]:
                        pair(0, False)
                    with pe.Fori(0 if b["act_done"] else 1, st.pairs) as i:
                        pair(i, True)
                elif st.kind == "tile":
                    if st.what == "out":
                        after(pe, x_lo_done, b["x_lo"])
                    after(pe, evac_act, b["evac_act"])
                    after(pe, evac_dve, b["evac_dve"])
                    free = evac_dve if st.half else evac_act
                    base = b["evac_dve"] if st.half else b["evac_act"]
                    if st.what == "down":
                        after(pe, h_lo_done, b["h_lo"])

                    def tiles(i, begun):
                        for s in range(2):
                            if begun:
                                pe.wait_ge(free, base + 2 * i + s - 1)
                            pe.wait_ge(w_split, b["w"] + 2 * i + s + 1)
                            bank = (4 + 2 * s, 5 + 2 * s)
                            if st.what == "down":
                                ins = products(s, same(FH), moving(h_hi), moving(h_lo), bank)
                            elif st.what == "out":
                                ins = products(s, same(DC), moving(xt_hi), moving(xt_lo), bank)
                            else:
                                pe.wait_ge(d_lo_done, b["d_lo"] - DC + 2 * i + 2)
                                def of(t):
                                    return lambda c, half: t[:, bass.ds(2 * i + c, 1), half * HALF:(half + 1) * HALF]
                                ins = products(s, same(2), of(h_hi), of(h_lo), bank)
                            ins.then_inc(acc_full, 1)
                    tiles(0, False)
                    with pe.Fori(1, DC // 2) as i:
                        tiles(i, True)
                elif st.kind == "attention":
                    after(pe, x_lo_done, b["x_lo"])
                    after(pe, evac_dve, b["evac_dve"])
                    attend(pe, st, products, moving)

_INS = ["x_prompt", "x_sample", "cache_k", "cache_v", "state_pool", "p_prompt", "p_sample", "ln_g", "ln_b", "ffn_w1",
        "ffn_w3", "ffn_w2", "pool_w", "pool_scale", "sb_w_in", "sb_w_out", "ple_w_gate", "ple_b_gate", "ple_w_proj"]
_OUTS = [(1, SEQ, D_MODEL), (DEC_BATCH, DEC_SEQ, D_MODEL), (1, 1, SEQ, HEADS, HEAD_DIM), (1, 1, SEQ, HEADS, HEAD_DIM),
         (1, DEC_BATCH, DEC_SEQ, HEADS, HEAD_DIM), (1, DEC_BATCH, DEC_SEQ, HEADS, HEAD_DIM), (1, 1, PREV, D_MODEL),
         (1, DEC_BATCH, PREV, D_MODEL)]


def kernel(**inputs):
    import numpy as _np
    import concourse.bacc as _bacc
    from concourse import mybir as _mybir
    from concourse.bass_utils import run_bass_kernel_spmd as _run

    nc = _bacc.Bacc("TRN2", target_bir_lowering=False, num_devices=1)
    arrays, args = {}, []
    for name in _INS:
        a = _np.ascontiguousarray(inputs[name])
        arrays[f"in_{name}_dram"] = a
        args.append(nc.dram_tensor(f"in_{name}_dram", a.shape, _mybir.dt.from_np(a.dtype), kind="ExternalInput").ap())
    for n, shape in enumerate(_OUTS):
        args.append(nc.dram_tensor(f"out_{n}_dram", shape, _mybir.dt.float32, kind="ExternalOutput").ap())
    streaming_trunk(nc, *args)
    r = _run(nc, [arrays], core_ids=[0])
    return tuple(r.results[0][f"out_{n}_dram"] for n in range(len(_OUTS)))
```

```python
from contextlib import ExitStack

import concourse.bass as bass
from concourse import mybir

P = 128
D_MODEL = 1024
SEQ = 512
DEPTH = 2
DEC_BATCH = 8
DEC_SEQ = 16
PAST = 1024
HEADS = 16
HEAD_DIM = D_MODEL // HEADS
WINDOWS = (2, 4, 8, 16)
PREV = max(WINDOWS) - 1
SCALED_BY_POOL = 4
D_FF = 2816
PLE = 256
ALPHA = (2.0 * DEPTH) ** 0.25
EPS = 1e-5
SCALE = HEAD_DIM ** -0.5
MASKED = -(2.0 ** 99)

TOKENS = SEQ + DEC_BATCH * DEC_SEQ
TILES = TOKENS // P
PROMPT_TILES = SEQ // P
HALF = TOKENS // 2
DC = D_MODEL // P
FC = D_FF // P
FH = FC // 2
PAIRS = HEADS // 2
SLOT = 12
KEY_BLOCKS = PAST // P

F32 = mybir.dt.float32
F32R = mybir.dt.float32r
I32 = mybir.dt.int32
SIGN = -(1 << 31)
ALU = mybir.AluOpType
ACT = mybir.ActivationFunctionType

UNITS = [("p", 0, 0), ("p", 1, 0), ("p", 0, 1), ("s", 0), ("p", 1, 1), ("s", 1), ("p", 0, 2), ("s", 2), ("p", 1, 2),
         ("s", 3)]
NU = len(UNITS)
SAMPLE_AT = [u for u, unit in enumerate(UNITS) if unit[0] == "s"]
PART_AT = (0, 512, 896)
PART_COLS = (512, 384, 512)
SB = 4
AUX = (13, 14)
CONVERT_AT = (6, 9)
TOTALS_USE = 7


def keys_uses(which, su):
    return 5 + 2 * (su + 1) + (1 if which == 1 and su else 0)


class Stage:

    def __init__(self, kind, chunks=(0, 0), what="", layer=0, n=0, half=0, pairs=0, then=""):
        self.kind, self.chunks, self.what, self.layer = kind, chunks, what, layer
        self.n, self.half, self.pairs, self.then = n, half, pairs, then
        self.base = {}
        self.landed = 0
        self.after = None


def plan_stages():
    stages = []

    def add(kind, chunks=(0, 0), **more):
        stages.append(Stage(kind, chunks, **more))

    def ffn(layer, n):
        for half in range(2):
            add("pair", (DC, DC), pairs=FH, what="ffn", layer=layer, n=n, half=half)
            if n == 1 and half == 1:
                add("ple", layer=layer)
            add("tile", (FH, FH), what="down", layer=layer, n=n, half=half)

    add("norm", what="load", then="split", layer=0, n=0)
    for layer in range(DEPTH):
        pool = layer % 2 == 0
        last = layer == DEPTH - 1
        ffn(layer, 0)
        add("norm", what="norm", layer=layer, n=0, then="window" if pool else "split")
        if pool:
            add("tile", (2, 2), what="pool", layer=layer, half=0)
        else:
            add("attention", (SLOT, SLOT), layer=layer)
            add("tile", (DC, DC), what="out", layer=layer, half=0)
        add("norm", what="norm", layer=layer, n=1, then="split")
        ffn(layer, 1)
        add("norm", what="norm", layer=layer, n=2, then="split")
        add("pair", (DC, PLE // P), pairs=DC, what="ple", layer=layer)
        add("norm", what="norm", layer=layer, n=3, then="none" if last else "split")

    value = {}
    for st in stages:
        st.base = {k: value.get(k, 0) for k in NAMES}
        for k, v in increments(st).items():
            value[k] = value.get(k, 0) + v
    for st, nxt in zip(stages, stages[1:] + [None]):
        after = [s for s in stages[stages.index(st) + 1:] if s.chunks[0]]
        st.after = after[0].chunks if after else None
    return stages


def after(engine, semaphore, value):
    if value:
        engine.wait_ge(semaphore, value)


def adds_late(st):
    return st.what == "norm" and st.n == 1


NAMES = ["w", "gate_full", "up_full", "act_done", "prod_done", "h_hi", "h_lo", "acc_full", "evac_act", "evac_dve",
         "yt_full", "res_done", "stat", "std", "x_norm", "xt_full", "x_hi", "x_lo", "gb", "x_hat", "scaled", "res_step", "pt_full",
         "pt_hi", "pt_lo"]


def increments(st):
    if st.kind == "pair":
        n = dict.fromkeys(["gate_full", "up_full", "act_done", "prod_done"], st.pairs)
        if st.what == "ffn":
            n.update(h_hi=st.pairs, h_lo=st.pairs)
        else:
            n.update(res_step=2 * DC)
        return n | {"w": 2 * st.pairs}
    if st.kind == "tile":
        n = {"w": DC, "acc_full": DC, ("evac_dve" if st.half else "evac_act"): DC}
        if st.what == "down" and st.half == 0:
            n["res_step"] = 2 * DC
        return n
    if st.kind == "norm":
        n = {}
        if st.what == "norm":
            n = dict.fromkeys(["yt_full", "stat", "std", "x_hat", "x_norm"], TILES) | {"gb": 32, "scaled": SCALED_BY_POOL}
            if adds_late(st):
                n["res_done"] = TILES
        if st.then != "none":
            n.update(xt_full=TILES, x_hi=TILES, x_lo=TILES)
        return n
    if st.kind == "ple":
        return {"pt_full": 2, "pt_hi": 2, "pt_lo": 2}
    if st.kind == "attention":
        return {"w": 2 * PAIRS, "x_hi": DC, "x_lo": DC}
    raise ValueError(st.kind)


def streaming_trunk(nc, x_prompt, x_sample, cache_k, cache_v, state_pool, p_prompt, p_sample, ln_g, ln_b, ffn_w1,
                    ffn_w3, ffn_w2, pool_w, pool_scale, sb_w_in, sb_w_out, ple_w_gate, ple_b_gate, ple_w_proj,
                    y_prompt, y_sample, new_k_prompt, new_v_prompt, new_k_sample, new_v_sample, new_pool_prompt,
                    new_pool_sample):
    stages = plan_stages()
    attention = next(s for s in stages if s.kind == "attention")
    norms = [s for s in stages if s.kind == "norm" and s.what == "norm"]

    with ExitStack() as ctx:
        def sb(name, shape, dt=F32):
            return ctx.enter_context(nc.sbuf_tensor(name, shape, dt))

        def sem(name):
            return ctx.enter_context(nc.semaphore(name))

        x = sb("x", [P, TILES, D_MODEL])
        y_t = sb("y_t", [P, DC, TOKENS])
        w_raw = sb("w_raw", [P, 2, SLOT, P])
        w_hi = sb("w_hi", [P, 2, SLOT, P], F32R)
        w_lo = sb("w_lo", [P, 2, SLOT, P], F32R)
        act = sb("act", [P, TOKENS])
        ident = sb("ident", [P, P])
        ident_r = sb("ident_r", [P, P], F32R)
        neg_tri = sb("neg_tri", [P, P])
        neg_ones = sb("neg_ones", [P, P])
        mask_f = sb("mask_f", [P, 2, P])
        mask_r = sb("mask_r", [P, 2, P], F32R)
        eps = sb("eps", [P, 1])
        one = sb("one", [P, 1])
        stats = sb("stats", [P, TILES, 12])
        mv = sb("mv", [P, TILES, 2])
        std = sb("std", [P, TILES])
        rstd = sb("rstd", [P, TILES])
        shift = sb("shift", [P, TILES])
        gate_b = sb("gate_b", [P, DEPTH, DC])
        scale_p = sb("scale_p", [P, DC])

        at_xt = ctx.enter_context(nc.sbuf_tensor("region_xt", [P, 2 * DC * TOKENS], F32))
        at_gb = ctx.enter_context(nc.sbuf_tensor("region_gb", [P, 2 * D_MODEL], F32))
        arena_bytes = 76320
        at_arena = ctx.enter_context(nc.sbuf_tensor("region_arena", [P, arena_bytes // 4], F32))
        sizes = {at_xt.name: 8 * DC * TOKENS, at_gb.name: 8 * D_MODEL, at_arena.name: arena_bytes}
        used = {}

        def place(where, name, shape, dt=F32, at=None):
            nbytes = 4
            for n in shape[1:]:
                nbytes *= n
            start = used.get(where.name, 0) if at is None else at
            used[where.name] = start + nbytes
            assert used[where.name] <= sizes[where.name], (name, used[where.name], sizes[where.name])
            base = nc.lookup_mls(where.name).memorylocations[0].addr
            return nc.alloc_sbuf_tensor_at(name, shape, dt, offset=base + start)

        xt_hi = place(at_xt, "xt_hi", [P, DC, TOKENS], F32R)
        xt_lo = place(at_xt, "xt_lo", [P, DC, TOKENS], F32R)
        band = place(at_xt, "band", [P, len(WINDOWS), 3, P], at=0)
        band_prev = place(at_xt, "band_prev", [P, len(WINDOWS), P])
        band_state = place(at_xt, "band_state", [P, len(WINDOWS), P])
        state_t = place(at_xt, "state_t", [DEC_BATCH * PREV, D_MODEL])

        g_b = place(at_gb, "g_b", [P, D_MODEL])
        b_b = place(at_gb, "b_b", [P, D_MODEL])
        q_t = place(at_gb, "q_t", [P, TOKENS], at=0)
        k_t = place(at_gb, "k_t", [P, TOKENS])
        k_tok = place(at_gb, "k_tok", [P, TILES, P])

        h_hi = place(at_arena, "h_hi", [P, FH, TOKENS], F32R)
        h_lo = place(at_arena, "h_lo", [P, FH, TOKENS], F32R)
        p_tok = place(at_arena, "p_tok", [P, TILES, PLE])
        p_hi = place(at_arena, "p_hi", [P, PLE // P, TOKENS], F32R)
        p_lo = place(at_arena, "p_lo", [P, PLE // P, TOKENS], F32R)
        k_raw = place(at_arena, "k_raw", [P, 2, SB, SB, P], at=0)
        v_raw = place(at_arena, "v_raw", [P, 2, SB, SB, P])
        kc_t = place(at_arena, "kc_t", [P, SB, SB, P])
        sp_p = place(at_arena, "sp_p", [P, 2, sum(PART_COLS)])
        relu_s = place(at_arena, "relu_s", [P, 2, 512])
        s_sum = place(at_arena, "s_sum", [P, 2, 512])
        total = place(at_arena, "total", [P, 8])
        e_buf = place(at_arena, "e_buf", [P, 2, 512])
        wt = place(at_arena, "wt", [P, 3, 512])
        q_blk = place(at_arena, "q_blk", [P, DEC_BATCH, 2, DEC_SEQ])
        v_tok = place(at_arena, "v_tok", [P, TILES, P])
        own_sp = place(at_arena, "own_sp", [P, DEC_BATCH, 2, DEC_SEQ])
        o_past = place(at_arena, "o_past", [P, 2, P])
        v_t = act
        o_t = y_t
        ps = ctx.enter_context(nc.psum_tensor("ps", [P, 8, 512], F32))

        const_step = sem("const_step")
        const_r = sem("const_r")
        x_loaded = sem("x_loaded")
        small_loaded = sem("small_loaded")
        w_loaded = [sem("w_loaded0"), sem("w_loaded1")]
        w_hi_done = sem("w_hi_done")
        w_split = sem("w_split")
        gate_full = sem("gate_full")
        up_full = sem("up_full")
        act_done = sem("act_done")
        prod_done = sem("prod_done")
        h_hi_done = sem("h_hi_done")
        h_lo_done = sem("h_lo_done")
        acc_full = sem("acc_full")
        evac_act = sem("evac_act")
        evac_dve = sem("evac_dve")
        yt_full = sem("yt_full")
        res_done = sem("res_done")
        stat_done = sem("stat_done")
        std_done = sem("std_done")
        shift_done = sem("shift_done")
        x_hat_done = sem("x_hat_done")
        scaled = sem("scaled")
        x_norm = sem("x_norm")
        res_step = sem("res_step")
        xt_full = sem("xt_full")
        x_hi_done = sem("x_hi_done")
        x_lo_done = sem("x_lo_done")
        gb_loaded = sem("gb_loaded")
        dve_step = sem("dve_step")
        state_loaded = sem("state_loaded")
        band_step = sem("band_step")
        p_loaded = sem("p_loaded")
        pt_full = sem("pt_full")
        pt_hi_done = sem("pt_hi_done")
        pt_lo_done = sem("pt_lo_done")
        k_loaded = [sem("k_loaded0"), sem("k_loaded1")]
        v_loaded = [sem("v_loaded0"), sem("v_loaded1")]
        aux_full = [sem("aux_full_a"), sem("aux_full_v")]
        aux_free = [sem("aux_free_a"), sem("aux_free_v")]
        q_blk_zero = sem("q_blk_zero")
        q_blk_done = sem("q_blk_done")
        z_full = sem("z_full")
        na_done = sem("na_done")
        el_done = sem("el_done")
        sp_done = sem("sp_done")
        own_copied = sem("own_copied")
        relu_done = sem("relu_done")
        arg_done = sem("arg_done")
        w_rows_done = sem("w_rows_done")
        past_saved = sem("past_saved")
        past_full = sem("past_full")
        s_full = sem("s_full")
        wt_done = sem("wt_done")
        pv_done = sem("pv_done")
        ot_act = sem("ot_act")
        ot_dve = sem("ot_dve")
        kv_stored = sem("kv_stored")
        pool_stored = sem("pool_stored")
        y_stored = sem("y_stored")

        xp = x_prompt[0].rearrange("(t p) d -> p t d", p=P)
        xs = x_sample.rearrange("b s d -> (b s) d")

        def block_source(st, s, i):
            if st.kind == "pair" and st.what == "ffn":
                w = (ffn_w1, ffn_w3)[s][st.layer, st.n].rearrange("(c p) f -> p c f", p=P)
                return [(0, DC, w[:, :, bass.ds(i * P + st.half * FH * P, P)])]
            if st.kind == "pair":
                w = (ple_w_gate, ple_w_proj)[s][st.layer].rearrange("(c p) f -> p c f", p=P)
                return [(0, st.chunks[s], w[:, :, bass.ds(i * P, P)])]
            if st.kind == "tile" and st.what == "down":
                w = ffn_w2[st.layer, st.n].rearrange("(c p) f -> p c f", p=P)
                return [(0, FH, w[:, st.half * FH:(st.half + 1) * FH, bass.ds(i * 2 * P + s * P, P)])]
            if st.kind == "tile" and st.what == "out":
                w = sb_w_out[0].rearrange("(c p) f -> p c f", p=P)
                return [(0, DC, w[:, :, bass.ds(i * 2 * P + s * P, P)])]
            if st.kind == "tile":
                w = pool_w[0].rearrange("g (c p) f -> p g c f", p=P)
                return [(0, 2, w[:, i, :, s * P:(s + 1) * P])]
            w = sb_w_in[0].rearrange("(c p) (m f) -> p c m f", p=P, m=3)
            col = bass.ds(i * P, P)
            if s == 0:
                return [(0, DC, w[:, :, 0, col]), (DC, 4, w[:, 0:4, 2, col])]
            return [(0, 4, w[:, 4:8, 2, col]), (4, DC, w[:, :, 1, col])]

        def block_loads(st):
            return 32 if st.kind == "attention" else 16

        def iterations(st):
            return st.pairs if st.kind == "pair" else PAIRS if st.kind == "attention" else DC // 2

        landed = 0
        for st in stages:
            if st.chunks[0]:
                st.landed = landed
                landed += block_loads(st) * iterations(st)

        def after_stage(st):
            later = [s for s in stages[stages.index(st) + 1:] if s.chunks[0]]
            return later[0] if later else None

        kc = cache_k[0].rearrange("b (k p) h d -> p b k (h d)", p=P)
        vc = cache_v[0].rearrange("b (k p) h d -> p b k (h d)", p=P)

        def attend_pool(pool, st):
            after(pool, evac_dve, st.base["evac_dve"])
            pool.memset(q_blk[:], 0.0).then_inc(q_blk_zero, 1)
            k_out = new_k_prompt[0, 0].rearrange("(t p) h d -> p t (h d)", p=P)
            v_out = new_v_prompt[0, 0].rearrange("(t p) h d -> p t (h d)", p=P)
            ks_out = new_k_sample[0].rearrange("b s h d -> (b s) (h d)")
            vs_out = new_v_sample[0].rearrange("b s h d -> (b s) (h d)")
            with pool.Fori(0, PAIRS) as i:
                col = bass.ds(i * P, P)
                pool.wait_ge(aux_free[0], AUX[0] * i + 5)
                pool.wait_ge(aux_free[1], AUX[1] * i + 5)
                pool.dma_start(k_out[:, :, col], k_tok[:, 0:PROMPT_TILES, :]).then_inc(kv_stored, 16)
                pool.dma_start(ks_out[:, col], k_tok[:, PROMPT_TILES, :]).then_inc(kv_stored, 16)
                pool.dma_start(v_out[:, :, col], v_tok[:, 0:PROMPT_TILES, :]).then_inc(kv_stored, 16)
                pool.dma_start(vs_out[:, col], v_tok[:, PROMPT_TILES, :]).then_inc(kv_stored, 16)

        def cols_of(u):
            return PART_COLS[UNITS[u][2]] if UNITS[u][0] == "p" else 512

        def attend(pe, st, products, moving):
            b = st.base

            def mm(out, w, xx, start=False):
                return pe.matmul(out, w, xx, start=start, stop=True, skip_group_check=True)

            uses = [0, 0]

            def aux_wait(i, which):
                if not isinstance(i, int) or AUX[which] * i + uses[which]:
                    pe.wait_ge(aux_free[which], AUX[which] * i + uses[which])
                uses[which] += 1

            def project(i, parts):
                aux_wait(i, 0)
                aux_wait(i, 1)
                for n, (s, chunks) in enumerate(parts):
                    for half in range(2):
                        ins = products(s, chunks, moving(xt_hi), moving(xt_lo), (6, 7), first=(n == 0),
                                       last=(n == len(parts) - 1), only=(half,))
                        if n == len(parts) - 1:
                            ins.then_inc(aux_full[half], 1)

            def project_q(i):
                uses[:] = [0, 0]
                pe.wait_ge(w_split, b["w"] + 2 * i + 1)
                project(i, [(0, [(c, c) for c in range(8)])])

            def project_v(i):
                pe.wait_ge(w_split, b["w"] + 2 * i + 2)
                project(i, [(0, [(8 + c, c) for c in range(4)]), (1, [(c, 4 + c) for c in range(4)])])

            def project_k(i):
                pe.wait_ge(w_split, b["w"] + 2 * i + 2)
                project(i, [(1, [(4 + c, c) for c in range(8)])])

            def to_tokens(i, src, evacuated):
                for which in range(2):
                    pe.wait_ge(aux_free[which], AUX[which] * i + evacuated)
                aux_wait(i, 0)
                for t in range(PROMPT_TILES):
                    ins = pe.transpose(ps[:, 6, t * P:(t + 1) * P], src[:, t * P:(t + 1) * P], ident[:])
                ins.then_inc(aux_full[0], 1)
                aux_wait(i, 1)
                pe.transpose(ps[:, 7, 0:P], src[:, SEQ:], ident[:]).then_inc(aux_full[1], 1)

            def transpose_past(i):
                pe.wait_ge(past_saved, i + 1)
                for g in range(2):
                    ins = pe.transpose(ps[:, 5, (1 + g) * P:(2 + g) * P], o_past[:, g, :], ident[:])
                ins.then_inc(past_full, 1)

            def pair_of_heads(i, begun, last):
                def cached_keys(su):
                    slot = su % 2
                    pe.wait_ge(k_loaded[slot], 128 * i + 64 * (su // 2) + 64)
                    for j in range(SB):
                        which = j % 2
                        aux_wait(i, which)
                        for kb in range(SB):
                            ins = pe.transpose(ps[:, 6 + which, kb * P:(kb + 1) * P], k_raw[:, slot, j, kb, :], ident[:])
                        ins.then_inc(aux_full[which], 1)

                def own_totals():
                    pe.wait_ge(own_copied, 2 * i + 2)
                    aux_wait(i, 1)
                    for b8 in range(DEC_BATCH):
                        g, j = divmod(b8, SB)
                        ins = mm(ps[32 * j:32 * (j + 1), 7, g:g + 1],
                                 own_sp[:, b8].rearrange("p h s -> p (h s)"), one[:, 0:1], start=True)
                    ins.then_inc(aux_full[1], 1)

                def scores(u):
                    if u >= 4:
                        pe.wait_ge(wt_done, NU * i + u - 3)
                    z = ps[:, u % 4, :]
                    if UNITS[u][0] == "p":
                        _, h, part = UNITS[u]
                        rows = slice(HEAD_DIM * h, HEAD_DIM * (h + 1))
                        blocks = {0: [(3, 0, 0), (2, P, 0), (4, 3 * P, 1)], 1: [(1, 0, 0)], 2: [(0, 0, 0)]}[part]
                        first = True
                        for kb, at, mask in blocks:
                            stop = TOKENS if kb == 4 else SEQ
                            n = stop - kb * P
                            mm(z[:, at:at + n], k_t[rows, kb * P:(kb + 1) * P], q_t[rows, kb * P:stop], start=first)
                            ins = mm(z[:, at:at + P], ident_r[:], mask_r[:, mask, :])
                            first = False
                    else:
                        su = UNITS[u][1]
                        pe.wait_ge(q_blk_done, 2 * i + 2)
                        for which in range(2):
                            pe.wait_ge(aux_free[which], AUX[which] * i + keys_uses(which, su))
                        for j in range(SB):
                            ins = mm(ps[32 * j:32 * (j + 1), u % 4, :],
                                     q_blk[:, SB * (su // 2) + j].rearrange("p h s -> p (h s)"),
                                     kc_t[:, j].rearrange("p k n -> p (k n)"), start=True)
                    ins.then_inc(z_full, 1)

                def suffix(u):
                    z = ps[:, u % 4, :]
                    if UNITS[u][0] == "p":
                        pe.wait_ge(sp_done, NU * i + u + 1)
                        _, h, part = UNITS[u]
                        sp = sp_p[:, h, :]
                        at, n = PART_AT[part], PART_COLS[part]
                        ins = mm(z[:, 0:n], neg_tri[:], sp[:, at:at + n])
                        kb3, kb2, kb1 = sp[:, 0:P], sp[:, P:3 * P], sp[:, 512:896]
                        later = {0: [(2 * P, 3 * P, kb3)], 1: [(P, 3 * P, kb2), (2 * P, 3 * P, kb3)],
                                 2: [(P, 4 * P, kb1), (2 * P, 4 * P, kb2), (3 * P, 4 * P, kb3)]}[part]
                        for lo, hi, src in later:
                            ins = mm(z[:, lo:hi], neg_ones[:], src)
                    else:
                        su = UNITS[u][1]
                        pe.wait_ge(w_rows_done, 4 * i + su + 1)
                        for kb in range(SB):
                            ins = pe.transpose(z[:, kb * P:(kb + 1) * P], relu_s[:, su % 2, kb * P:(kb + 1) * P], ident[:])
                    ins.then_inc(s_full, 1)

                def values(u):
                    pe.wait_ge(wt_done, NU * i + u + 1)
                    if u == 0:
                        for which in range(2):
                            pe.wait_ge(aux_free[which], AUX[which] * i + 5)
                        if begun:
                            pe.wait_ge(ot_dve, i)
                    w = wt[:, u % 3, :]
                    if UNITS[u][0] == "p":
                        _, h, part = UNITS[u]
                        rows = slice(HEAD_DIM * h, HEAD_DIM * (h + 1))
                        v = lambda kb: v_tok[:, kb, rows]
                        if part == 0:
                            mm(ps[rows, 4, 3 * P:4 * P], v(3), w[:, 0:P], start=True)
                            mm(ps[rows, 4, 2 * P:4 * P], v(2), w[:, P:3 * P])
                            ins = mm(ps[rows, 5, 0:P], v(4), w[:, 3 * P:4 * P], start=True)
                        elif part == 1:
                            ins = mm(ps[rows, 4, P:4 * P], v(1), w[:, 0:3 * P])
                        else:
                            ins = mm(ps[rows, 4, :], v(0), w)
                    else:
                        su = UNITS[u][1]
                        slot = su % 2
                        pe.wait_ge(v_loaded[slot], 128 * i + 64 * (su // 2) + 64)
                        at = (1 + su // 2) * P
                        for kb in range(SB):
                            for j in range(SB):
                                ins = mm(ps[32 * j:32 * (j + 1), 5, at:at + P], w[:, kb * P + 32 * j:kb * P + 32 * (j + 1)],
                                         v_raw[:, slot, j, kb, :])
                    ins.then_inc(pv_done, 1)

                fill = {NU - 1: project_q, NU + 1: project_k}
                for u in range(NU + 4):
                    if u < NU:
                        if u == 0:
                            for which in range(2):
                                pe.wait_ge(aux_free[which], AUX[which] * i + 2)
                        scores(u)
                    if u == 0:
                        project_v(i)
                        if begun:
                            transpose_past(i - 1)
                    if u == 1:
                        to_tokens(i, k_t, 2)
                    if u == 2:
                        to_tokens(i, v_t, 3)
                    if u + 1 in SAMPLE_AT:
                        cached_keys(SAMPLE_AT.index(u + 1))
                    if u == 3:
                        own_totals()
                    if 2 <= u < NU + 2:
                        suffix(u - 2)
                    if u >= 4:
                        values(u - 4)
                    if u in fill and not last:
                        fill[u](i + 1)

            project_q(0)
            project_k(0)
            pair_of_heads(0, False, False)
            with pe.Fori(1, PAIRS - 1) as i:
                pair_of_heads(i, True, False)
            pair_of_heads(PAIRS - 1, True, True)
            transpose_past(PAIRS - 1)

        block = ctx.enter_context(nc.Block())

        @block.sync
        def _(sp):
            for t in range(PROMPT_TILES):
                sp.dma_start(x[:, t, :], xp[:, t, :]).then_inc(x_loaded, 16)
            sp.dma_start(x[:, PROMPT_TILES, :], xs).then_inc(x_loaded, 16)

            def load_blocks(st, i, wait=True):
                for s in range(2):
                    if wait:
                        sp.wait_ge(w_split, st.base["w"] + 2 * i + s - 1)
                    for c0, n, src in block_source(st, s, i):
                        sp.dma_start(w_raw[:, s, c0:c0 + n, :], src).then_inc(w_loaded[s], 16)

            def sample_slices(su):
                return SB * (su // 2), slice(SB, 2 * SB) if su % 2 == 0 else slice(0, SB)

            def load_keys(i, su):
                slot = su % 2
                batch, blocks = sample_slices(su)
                if su >= 2:
                    sp.wait_ge(aux_full[1], AUX[1] * i + keys_uses(1, su - 2))
                elif not isinstance(i, int) or i:
                    sp.wait_ge(aux_full[1], AUX[1] * i - AUX[1] + keys_uses(1, su + 2))
                for j in reversed(range(SB)):
                    sp.dma_start(k_raw[:, slot, j], kc[:, batch + j, blocks, bass.ds(i * P, P)]).then_inc(k_loaded[slot], 16)

            def load_values(i, su):
                slot = su % 2
                batch, blocks = sample_slices(su)
                if su >= 2:
                    sp.wait_ge(pv_done, NU * i + SAMPLE_AT[su - 2] + 1)
                elif not isinstance(i, int) or i:
                    sp.wait_ge(pv_done, NU * i - NU + SAMPLE_AT[su + 2] + 1)
                for j in range(SB):
                    sp.dma_start(v_raw[:, slot, j], vc[:, batch + j, blocks, bass.ds(i * P, P)]).then_inc(v_loaded[slot], 16)

            for st in stages:
                if not st.chunks[0]:
                    continue
                if st.kind != "attention":
                    if st.base["w"] == 0:
                        load_blocks(st, 0, wait=False)
                    with sp.Fori(1 if st.base["w"] == 0 else 0, iterations(st)) as i:
                        load_blocks(st, i)
                    continue
                load_blocks(st, 0)
                load_blocks(st, 1)
                after(sp, evac_dve, st.base["evac_dve"])
                load_keys(0, 0)
                for su in range(4):
                    load_keys((su + 1) // 4, (su + 1) % 4)
                    load_values(0, su)
                with sp.Fori(1, PAIRS - 1) as i:
                    load_blocks(st, i + 1)
                    for su in range(4):
                        load_keys(i + (su + 1) // 4, (su + 1) % 4)
                        load_values(i, su)
                for su in range(4):
                    if su < 3:
                        load_keys(PAIRS - 1, su + 1)
                    load_values(PAIRS - 1, su)

        @block.gpsimd
        def _(pool):
            step = [0]

            def link(ins):
                step[0] += 1
                ins.then_inc(const_step, 1)
                pool.wait_ge(const_step, step[0])

            pool.dma_start(gate_b[:, :, :], ple_b_gate.rearrange("l (c p) -> p l c", p=P),
                           allow_slow_non_contiguous=True).then_inc(small_loaded, 16)
            pool.dma_start(scale_p[:, :], pool_scale[0].rearrange("(c p) -> p c", p=P),
                           allow_slow_non_contiguous=True).then_inc(small_loaded, 16)

            def load_gb(st):
                for dst, src in ((g_b, ln_g), (b_b, ln_b)):
                    row = src[st.layer, st.n:st.n + 1, :]
                    pool.dma_start(dst[:, :], row.broadcast_to([P, D_MODEL])).then_inc(gb_loaded, 16)

            def load_p(layer):
                pool.dma_start(p_tok[:, 0:PROMPT_TILES, :],
                               p_prompt[layer, 0].rearrange("(t p) d -> p t d", p=P)).then_inc(p_loaded, 16)
                pool.dma_start(p_tok[:, PROMPT_TILES, :],
                               p_sample[layer].rearrange("b s d -> (b s) d")).then_inc(p_loaded, 16)

            def build_bands():
                nw = len(WINDOWS)
                steps = [0]

                def link(ins):
                    steps[0] += 1
                    ins.then_inc(band_step, 1)
                    pool.wait_ge(band_step, steps[0])

                def keep(view, base, pattern, slope):
                    return pool.affine_select(out=view, in_=view, compare_op=ALU.is_ge, fill=0.0, base=base,
                                              pattern=pattern, channel_multiplier=slope)

                for k, w in enumerate(WINDOWS):
                    pool.memset(band[:, k], 1.0 / w)
                    pool.memset(band_prev[:, k], 1.0 / w)
                    ins = pool.memset(band_state[:, k], 1.0 / w)
                link(ins)
                for t in range(PREV):
                    k = next(k for k, w in enumerate(WINDOWS) if w > t + 1)
                    ins = pool.memset(band[:, k:, 0, t:t + 1], 1.0 / (t + 1))
                link(ins)
                for k, w in enumerate(WINDOWS):
                    keep(band[:, k], 0, [[0, 3], [1, P]], -1)
                    keep(band_prev[:, k], w - 1 - P, [[-1, P]], 1)
                    ins = keep(band_state[:, k], w - 1 - PREV, [[-PREV, DEC_BATCH], [-1, DEC_SEQ]], 1)
                link(ins)
                for k, w in enumerate(WINDOWS):
                    keep(band[:, k], w - 1, [[0, 3], [-1, P]], 1)
                    ins = keep(band_state[:, k], PREV - 1, [[PREV, DEC_BATCH], [0, DEC_SEQ]], -1)
                link(ins)
                for k in range(nw):
                    ins = keep(band[:, k, 2], 0, [[-DEC_SEQ, DEC_BATCH], [0, DEC_SEQ]], 1)
                link(ins)
                for k in range(nw):
                    for kind in range(3):
                        ins = pool.tensor_tensor(band[:, k, kind], band[:, k, kind], ident[:], ALU.subtract)
                link(ins)

            load_gb(norms[0])
            load_p(0)
            pool.memset(ident[:], 0.0)
            pool.memset(neg_tri[:], -1.0)
            pool.memset(neg_ones[:], -1.0)
            pool.memset(eps[:], EPS)
            pool.memset(one[:], 1.0)
            link(pool.memset(mask_f[:], 0.0))
            link(pool.affine_select(out=ident[:], in_=ident[:], compare_op=ALU.not_equal, fill=1.0, base=0,
                                    pattern=[[-1, P]], channel_multiplier=1))
            link(pool.affine_select(out=neg_tri[:], in_=neg_tri[:], compare_op=ALU.is_ge, fill=0.0, base=0,
                                    pattern=[[-1, P]], channel_multiplier=1))
            link(pool.affine_select(out=mask_f[:], in_=mask_f[:], compare_op=ALU.is_gt, fill=MASKED, base=0,
                                    pattern=[[0, 2], [1, P]], channel_multiplier=-1))
            own = mask_f[:, 1, :].rearrange("p (b s) -> p b s", s=DEC_SEQ)
            link(pool.affine_select(out=own, in_=own, compare_op=ALU.is_ge, fill=MASKED, base=0,
                                    pattern=[[-DEC_SEQ, DEC_BATCH], [0, DEC_SEQ]], channel_multiplier=1))

            norm_index = 0
            for st in stages:
                b = st.base
                if st.kind == "norm" and st.what == "norm":
                    norm_index += 1
                    pool.wait_ge(gb_loaded, b["gb"] + 32)
                    for t in range(SCALED_BY_POOL):
                        pool.wait_ge(x_hat_done, b["x_hat"] + t + 1)
                        pool.tensor_tensor(x[:, t, :], x[:, t, :], g_b[:, :], ALU.mult).then_inc(scaled, 1)
                    pool.wait_ge(x_norm, b["x_norm"] + TILES)
                    if norm_index < len(norms) and norms[norm_index].base["w"] <= attention.base["w"]:
                        load_gb(norms[norm_index])
                    elif norm_index < len(norms) and st.base["w"] > attention.base["w"]:
                        load_gb(norms[norm_index])
                    if st.then == "window":
                        pool.dma_start(new_pool_prompt[0, 0], x[P - PREV:P, PROMPT_TILES - 1, :]).then_inc(pool_stored, 16)
                        for n in range(DEC_BATCH):
                            lo = (n + 1) * DEC_SEQ - PREV
                            pool.dma_start(new_pool_sample[0, n], x[lo:lo + PREV, PROMPT_TILES, :]).then_inc(pool_stored, 16)
                    if st.then == "none":
                        pool.dma_start(y_prompt[0].rearrange("(t p) d -> p t d", p=P),
                                       x[:, 0:PROMPT_TILES, :]).then_inc(y_stored, 16)
                        pool.dma_start(y_sample.rearrange("b s d -> (b s) d"),
                                       x[:, PROMPT_TILES, :]).then_inc(y_stored, 16)
                if st.kind == "tile" and st.what == "down" and st.half == 1 and st.layer == 0 and st.n == 0:
                    after(pool, up_full, b["up_full"])
                    after(pool, res_step, b["res_step"])
                    pool.dma_start(state_t[:, :], state_pool[0].rearrange("b r d -> (b r) d")).then_inc(state_loaded, 16)
                    build_bands()
                if st.kind == "attention":
                    attend_pool(pool, st)
                    pool.wait_ge(kv_stored, 64 * PAIRS)
                    pool.wait_ge(ot_dve, PAIRS)
                    load_gb(norms[norm_index])
                    load_p(1)
            pool.wait_ge(pool_stored, 16 * (1 + DEC_BATCH))
            pool.wait_ge(kv_stored, 64 * PAIRS)
            pool.wait_ge(y_stored, 32)

        @block.scalar
        def _(se):
            def cvt(st, n, s, landed_at):
                k = st.chunks[s]
                se.wait_ge(w_loaded[s], landed_at)
                se.activation(w_hi[:, s, 0:k, :], w_raw[:, s, 0:k, :], ACT.Copy).then_inc(w_hi_done, 1)

            def cvt_of(st, i, s):
                cvt(st, None, s, st.landed + block_loads(st) * (i + 1))

            def next_cvt(st, i, s, last):
                if not last:
                    cvt_of(st, i + 1, s)
                elif after_stage(st) is not None:
                    cvt_of(after_stage(st), 0, s)

            first = next(s for s in stages if s.chunks[0])

            for st in stages:
                b = st.base
                if st.kind == "norm":
                    for t in range(TILES + 3):
                        if t >= 3 and st.then != "none":
                            n = t - 3
                            bank = 4 + 2 * (n % 2)
                            se.wait_ge(xt_full, b["xt_full"] + n + 1)
                            tile = ps[:, bank:bank + 2, :].rearrange("p b n -> p (b n)")
                            hi = xt_hi[:, :, n * P:(n + 1) * P] if st.then == "split" else h_hi[:, 0:DC, n * P:(n + 1) * P]
                            se.activation(hi, tile.rearrange("p (c t) -> p c t", t=P), ACT.Copy).then_inc(x_hi_done, 1)
                        if t < TILES and st.what == "norm":
                            se.wait_ge(stat_done, b["stat"] + t + 1)
                            se.activation(std[:, t:t + 1], mv[:, t, 1:2], ACT.Sqrt, bias=eps[:, 0:1]).then_inc(std_done, 1)
                            bank = 2 * (t % 2)
                            u = x[:, t, :] if adds_late(st) else ps[:, bank:bank + 2, :].rearrange("p b n -> p (b n)")
                            se.wait_ge(shift_done, b["x_hat"] + t + 1)
                            se.activation(x[:, t, :], u, ACT.Identity, bias=shift[:, t:t + 1],
                                          scale=rstd[:, t:t + 1]).then_inc(x_hat_done, 1)
                    if st is stages[0]:
                        cvt_of(first, 0, 0)
                        cvt_of(first, 0, 1)
                elif st.kind == "ple":
                    for c in range(PLE // P):
                        se.wait_ge(pt_full, b["pt_full"] + c + 1)
                        se.activation(p_hi[:, c, :], ps[:, 4 + 2 * c:6 + 2 * c, :].rearrange("p b n -> p (b n)")[:, 0:TOKENS],
                                      ACT.Copy).then_inc(pt_hi_done, 1)
                elif st.kind == "pair":
                    def pair(i, last):
                        se.wait_ge(gate_full, b["gate_full"] + i + 1)
                        if st.what == "ple":
                            se.wait_ge(prod_done, b["prod_done"] + i)
                        elif not isinstance(i, int) or b["h_lo"] + i:
                            se.wait_ge(h_lo_done, b["h_lo"] + i)
                        gate = ps[:, 0:2, 0:HALF]
                        dst = act[:, :].rearrange("p (t n) -> p t n", t=2)
                        if st.what == "ffn":
                            se.activation(dst, gate, ACT.Silu).then_inc(act_done, 1)
                            next_cvt(st, i, 0, last)
                        else:
                            next_cvt(st, i, 0, last)
                            se.activation(dst, gate, ACT.Sigmoid,
                                          bias=gate_b[:, st.layer, bass.ds(i, 1)]).then_inc(act_done, 1)
                        if st.what == "ffn":
                            se.wait_ge(prod_done, b["prod_done"] + i + 1)
                            se.activation(h_hi[:, bass.ds(i, 1), :], act[:, :].rearrange("p (a n) -> p a n", a=1),
                                          ACT.Copy).then_inc(h_hi_done, 1)
                        se.wait_ge(up_full, b["up_full"] + i + 1)
                        next_cvt(st, i, 1, last)
                    if st.what == "ffn" and b["prod_done"]:
                        after(se, prod_done, b["prod_done"])
                    if st.what == "ple":
                        after(se, h_lo_done, b["h_lo"])
                        se.wait_ge(small_loaded, 32)
                    if st.what == "ffn":
                        se.preload_act_table(ACT.Silu)
                    else:
                        se.preload_act_table(ACT.Sigmoid)
                    if not b["h_lo"]:
                        pair(0, False)
                    with se.Fori(0 if b["h_lo"] else 1, st.pairs - 1) as i:
                        pair(i, False)
                    pair(st.pairs - 1, True)
                elif st.kind == "tile":
                    def tiles(i, last):
                        for s in range(2):
                            se.wait_ge(acc_full, b["acc_full"] + 2 * i + s + 1)
                            if st.half == 0:
                                src = ps[:, 4 + 2 * s:6 + 2 * s, 0:HALF]
                                dst = y_t[:, bass.ds(2 * i + s, 1), :].rearrange("p a (t n) -> p (a t) n", t=2)
                                if st.what == "pool":
                                    se.activation(dst, src, ACT.Copy, scale=scale_p[:, bass.ds(2 * i + s, 1)]).then_inc(evac_act, 1)
                                else:
                                    se.activation(dst, src, ACT.Copy, scale=0.5 if st.what == "down" else 1.0).then_inc(evac_act, 1)
                            next_cvt(st, i, s, last)
                    if st.what == "pool":
                        se.wait_ge(small_loaded, 32)
                    with se.Fori(0, DC // 2 - 1) as i:
                        tiles(i, False)
                    tiles(DC // 2 - 1, True)
                elif st.kind == "attention":
                    def aux(i, m, dst, scale=1.0, cols=512, tiled=False):
                        se.wait_ge(aux_full[0], AUX[0] * i + m + 1)
                        src = ps[:, 6, 0:cols]
                        if tiled:
                            src = src.rearrange("p (t n) -> p t n", n=P)
                        se.activation(dst, src, ACT.Copy, scale=scale).then_inc(aux_free[0], 1)

                    def weights(i, u):
                        se.wait_ge(s_full, NU * i + u + 1)
                        if u >= 3:
                            se.wait_ge(pv_done, NU * i + u - 2)
                        n = cols_of(u)
                        func = ACT.Exp if UNITS[u][0] == "p" else ACT.Copy
                        se.activation(wt[:, u % 3, 0:n], ps[:, u % 4, 0:n], func).then_inc(wt_done, 1)

                    def pair_of_heads(i, begun, last):
                        for u in range(NU + 2):
                            if u < NU:
                                n = cols_of(u)
                                e = e_buf[:, u % 2, 0:n]
                                se.wait_ge(na_done, NU * i + u + 1)
                                se.activation(e, e, ACT.Exp).then_inc(el_done, 1)
                                se.wait_ge(el_done, 2 * (NU * i + u) + 1)
                                se.activation(e, e, ACT.Ln, bias=1.0).then_inc(el_done, 1)
                            if u == 0:
                                aux(i, 2, v_t[:, 0:HALF], 1.0, HALF)
                            if u == 1:
                                if begun:
                                    se.wait_ge(kv_stored, 64 * i)
                                aux(i, 3, k_tok[:, 0:4, :], tiled=True)
                            if u == 2:
                                aux(i, 4, v_tok[:, 0:4, :], tiled=True)
                            if u + 1 in SAMPLE_AT:
                                su = SAMPLE_AT.index(u + 1)
                                for j in (0, 2):
                                    aux(i, 5 + 2 * su + j // 2, kc_t[:, j], tiled=True)
                            if u - 1 in SAMPLE_AT:
                                su = SAMPLE_AT.index(u - 1)
                                se.wait_ge(arg_done, 4 * i + su + 1)
                                se.activation(relu_s[:, su % 2, :], relu_s[:, su % 2, :], ACT.Exp).then_inc(w_rows_done, 1)
                            if u >= 2:
                                weights(i, u - 2)
                            if u in CONVERT_AT and not last:
                                next_cvt(st, i, CONVERT_AT.index(u), last)
                            if u == NU - 1 and not last:
                                aux(i + 1, 0, q_t[:, 0:HALF], SCALE, HALF)
                        if not last:
                            aux(i + 1, 1, k_t[:, 0:HALF], 1.0, HALF)
                        se.wait_ge(pv_done, NU * i + NU)
                        se.activation(o_t[:, bass.ds(i, 1), 0:SEQ], ps[:, 4:5, :], ACT.Copy)
                        se.activation(o_t[:, bass.ds(i, 1), SEQ:], ps[:, 5:6, 0:P], ACT.Copy).then_inc(ot_act, 1)
                        se.activation(o_past[:, :, :], ps[:, 5, P:3 * P].rearrange("p (g n) -> p g n", g=2),
                                      ACT.Copy).then_inc(past_saved, 1)

                    se.preload_act_table_set("natural_log_exp_and_others")
                    aux(0, 0, q_t[:, 0:HALF], SCALE, HALF)
                    aux(0, 1, k_t[:, 0:HALF], 1.0, HALF)
                    pair_of_heads(0, False, False)
                    with se.Fori(1, PAIRS - 1) as i:
                        pair_of_heads(i, True, False)
                    pair_of_heads(PAIRS - 1, True, True)
                    se.wait_ge(ot_dve, PAIRS)
                    for c in range(DC):
                        se.activation(xt_hi[:, c, :], o_t[:, c, :], ACT.Copy).then_inc(x_hi_done, 1)
                    for s in range(2):
                        next_cvt(st, PAIRS - 1, s, True)

        @block.vector
        def _(ve):
            step = [0]

            def link(ins):
                step[0] += 1
                ins.then_inc(dve_step, 1)
                ve.wait_ge(dve_step, step[0])

            def cvt(n, s, k):
                ve.wait_ge(w_hi_done, n + 1)
                ve.tensor_tensor(w_lo[:, s, 0:k, :], w_raw[:, s, 0:k, :], w_hi[:, s, 0:k, :].bitcast(F32),
                                 ALU.subtract).then_inc(w_split, 1)

            def next_cvt(st, i, s, last):
                if not last:
                    cvt(st.base["w"] + 2 * i + s + 2, s, st.chunks[s])
                elif st.after is not None:
                    cvt(st.base["w"] + 2 * i + s + 2, s, st.after[s])

            def add_residual(done, c):
                y = y_t[:, bass.ds(c, 1), :]
                for n, part in enumerate((xt_hi, xt_lo)):
                    ve.scalar_tensor_tensor(y, part[:, bass.ds(c, 1), :].bitcast(F32), ALPHA, y,
                                            ALU.mult, ALU.add).then_inc(res_step, 1)
                    if n == 0:
                        ve.wait_ge(res_step, done + 1)

            first = next(s for s in stages if s.chunks[0])
            ve.wait_ge(const_step, 5)
            ve.tensor_copy(ident_r[:], ident[:])
            ve.tensor_copy(mask_r[:], mask_f[:]).then_inc(const_r, 1)

            for st in stages:
                b = st.base
                if st.kind == "norm":
                    def residual(t):
                        bank = 2 * (t % 2)
                        u = ps[:, bank:bank + 2, :].rearrange("p b n -> p (b n)")
                        ve.wait_ge(yt_full, b["yt_full"] + t + 1)
                        if adds_late(st):
                            ve.scalar_tensor_tensor(x[:, t, :], x[:, t, :], ALPHA, u, ALU.mult, ALU.add).then_inc(res_done, 1)
                            ve.wait_ge(res_done, b["res_done"] + t + 1)
                            u = x[:, t, :]
                        ve.bn_stats(stats[:, t, 0:6], u[:, 0:512])
                        link(ve.bn_stats(stats[:, t, 6:12], u[:, 512:1024]))
                        ve.bn_aggr(mv[:, t, :], stats[:, t, :]).then_inc(stat_done, 1)

                    def shift_of(t):
                        ve.wait_ge(std_done, b["std"] + t + 1)
                        link(ve.reciprocal(rstd[:, t:t + 1], std[:, t:t + 1]))
                        ve.scalar_tensor_tensor(shift[:, t:t + 1], mv[:, t, 0:1], -1.0, rstd[:, t:t + 1],
                                                ALU.mult, ALU.mult).then_inc(shift_done, 1)

                    def normalise(t):
                        if t < SCALED_BY_POOL:
                            ve.wait_ge(scaled, b["scaled"] + t + 1)
                        else:
                            ve.wait_ge(x_hat_done, b["x_hat"] + t + 1)
                            link(ve.tensor_tensor(x[:, t, :], x[:, t, :], g_b[:, :], ALU.mult))
                        if t == 0:
                            ve.wait_ge(gb_loaded, b["gb"] + 32)
                        ve.tensor_tensor(x[:, t, :], x[:, t, :], b_b[:, :], ALU.add).then_inc(x_norm, 1)

                    def low(t):
                        bank = 4 + 2 * (t % 2)
                        ve.wait_ge(x_hi_done, b["x_hi"] + t + 1)
                        cols = slice(t * P, (t + 1) * P)
                        hi, lo = (xt_hi, xt_lo) if st.then == "split" else (h_hi, h_lo)
                        ve.tensor_tensor(lo[:, 0:DC, cols],
                                         ps[:, bank:bank + 2, :].rearrange("p b (c t) -> p (b c) t", t=P),
                                         hi[:, 0:DC, cols].bitcast(F32), ALU.subtract).then_inc(x_lo_done, 1)

                    if st.what == "norm" and stages[stages.index(st) - 1].kind == "tile" and st.n == 1 and st.layer == 0:
                        ve.wait_ge(pool_stored, 16 * (1 + DEC_BATCH))
                    for t in range(TILES + 3):
                        if t < TILES and st.what == "norm":
                            residual(t)
                        if t >= 3 and st.then != "none":
                            low(t - 3)
                        if t < TILES and st.what == "norm":
                            shift_of(t)
                        if 1 <= t <= TILES and st.what == "norm":
                            normalise(t - 1)
                    if st is stages[0]:
                        cvt(0, 0, first.chunks[0])
                        cvt(1, 1, first.chunks[1])
                elif st.kind == "ple":
                    for c in range(PLE // P):
                        ve.wait_ge(pt_hi_done, b["pt_hi"] + c + 1)
                        ve.tensor_tensor(p_lo[:, c, :], ps[:, 4 + 2 * c:6 + 2 * c, :].rearrange("p b n -> p (b n)")[:, 0:TOKENS],
                                         p_hi[:, c, :].bitcast(F32), ALU.subtract).then_inc(pt_lo_done, 1)
                elif st.kind == "pair":
                    def pair(i, last):
                        next_cvt(st, i, 0, last)
                        ve.wait_ge(act_done, b["act_done"] + i + 1)
                        ve.wait_ge(up_full, b["up_full"] + i + 1)
                        gate = act[:, :].rearrange("p (t n) -> p t n", t=2)
                        up = ps[:, 2:4, 0:HALF]
                        if st.what == "ffn":
                            ve.tensor_tensor(gate, gate, up, ALU.mult).then_inc(prod_done, 1)
                            ve.wait_ge(h_hi_done, b["h_hi"] + i + 1)
                            ve.tensor_tensor(h_lo[:, bass.ds(i, 1), :], act[:, :].rearrange("p (a n) -> p a n", a=1),
                                             h_hi[:, bass.ds(i, 1), :].bitcast(F32), ALU.subtract).then_inc(h_lo_done, 1)
                        else:
                            ve.tensor_tensor(y_t[:, bass.ds(i, 1), :].rearrange("p a (t n) -> p (a t) n", t=2),
                                             gate, up, ALU.mult).then_inc(prod_done, 1)
                        next_cvt(st, i, 1, last)
                        if st.what == "ple":
                            ve.wait_ge(prod_done, b["prod_done"] + i + 1)
                            add_residual(b["res_step"] + 2 * i, i)
                    if st.what == "ple":
                        after(ve, x_lo_done, b["x_lo"])
                    with ve.Fori(0, st.pairs - 1) as i:
                        pair(i, False)
                    pair(st.pairs - 1, True)
                elif st.kind == "tile":
                    def tiles(i, last):
                        for s in range(2):
                            if st.half == 1:
                                ve.wait_ge(acc_full, b["acc_full"] + 2 * i + s + 1)
                                dst = y_t[:, bass.ds(2 * i + s, 1), :].rearrange("p a (t n) -> p (a t) n", t=2)
                                ve.scalar_tensor_tensor(dst, ps[:, 4 + 2 * s:6 + 2 * s, 0:HALF], 0.5, dst,
                                                        ALU.mult, ALU.add).then_inc(evac_dve, 1)
                            next_cvt(st, i, s, last)
                            if st.half == 0 and st.what == "down":
                                ve.wait_ge(evac_act, b["evac_act"] + 2 * i + s + 1)
                                add_residual(b["res_step"] + 4 * i + 2 * s, 2 * i + s)
                    if st.half == 1:
                        after(ve, res_step, b["res_step"])
                        after(ve, evac_act, b["evac_act"])
                    with ve.Fori(0, DC // 2 - 1) as i:
                        tiles(i, False)
                    tiles(DC // 2 - 1, True)
                elif st.kind == "attention":
                    def aux(i, m, dst, scale=None, cols=512, tiled=False):
                        ve.wait_ge(aux_full[1], AUX[1] * i + m + 1)
                        src = ps[:, 7, 0:cols]
                        if tiled:
                            src = src.rearrange("p (t n) -> p t n", n=P)
                        if scale:
                            ve.tensor_scalar(dst, src, scale, None, ALU.mult).then_inc(aux_free[1], 1)
                        else:
                            ve.tensor_copy(dst, src).then_inc(aux_free[1], 1)

                    def evac_q(i):
                        aux(i, 0, q_t[:, HALF:], SCALE, HALF)
                        ve.wait_ge(aux_free[1], AUX[1] * i + 1)
                        for h in range(2):
                            rows = slice(HEAD_DIM * h, HEAD_DIM * (h + 1))
                            ve.tensor_copy(q_blk[rows, :, h, :],
                                           q_t[rows, SEQ:].rearrange("p (b s) -> p b s", s=DEC_SEQ)).then_inc(q_blk_done, 1)

                    def finish(i):
                        ve.wait_ge(ot_act, i + 1)
                        ve.wait_ge(past_full, i + 1)
                        for h in range(2):
                            rows = slice(HEAD_DIM * h, HEAD_DIM * (h + 1))
                            dst = o_t[rows, bass.ds(i, 1), SEQ:].rearrange("p a (b s) -> p (a b) s", s=DEC_SEQ)
                            past = ps[rows, 5, P:P + 2 * P].rearrange("p (b h s) -> p b h s", h=2, s=DEC_SEQ)[:, :, h, :]
                            ins = ve.tensor_tensor(dst, dst, past, ALU.add)
                        ins.then_inc(ot_dve, 1)

                    def pair_of_heads(i, begun, last):
                        def neg_abs(u):
                            n = cols_of(u)
                            ve.wait_ge(z_full, NU * i + u + 1)
                            if u >= 2:
                                ve.wait_ge(sp_done, NU * i + u - 1)
                            ve.tensor_scalar(e_buf[:, u % 2, 0:n].bitcast(I32), ps[:, u % 4, 0:n].bitcast(I32), SIGN, None,
                                             ALU.bitwise_or).then_inc(na_done, 1)
                            if UNITS[u][0] == "s":
                                su = UNITS[u][1]
                                if su >= 2:
                                    ve.wait_ge(s_full, NU * i + SAMPLE_AT[su - 2] + 1)
                                ve.tensor_scalar(relu_s[:, su % 2, :], ps[:, u % 4, :], 0.0, None,
                                                 ALU.max).then_inc(relu_done, 1)

                        def softplus(u):
                            n = cols_of(u)
                            ve.wait_ge(el_done, 2 * (NU * i + u) + 2)
                            at = PART_AT[UNITS[u][2]]
                            dst = sp_p[:, UNITS[u][1], at:at + n]
                            ve.scalar_tensor_tensor(dst, ps[:, u % 4, 0:n], 0.0, e_buf[:, u % 2, 0:n],
                                                    ALU.max, ALU.add).then_inc(sp_done, 1)
                            if u == 1:
                                ve.wait_ge(sp_done, NU * i + 2)
                                for h in range(2):
                                    ve.tensor_copy(own_sp[:, :, h, :],
                                                   sp_p[:, h, 3 * P:4 * P].rearrange("p (b s) -> p b s", s=DEC_SEQ)
                                                   ).then_inc(own_copied, 1)

                        def suffix(u):
                            su = UNITS[u][1]
                            slot = su % 2
                            ve.wait_ge(el_done, 2 * (NU * i + u) + 2)
                            ve.wait_ge(relu_done, 4 * i + su + 1)
                            if su == 0:
                                ve.wait_ge(aux_free[1], AUX[1] * i + TOTALS_USE + 1)
                            else:
                                ve.wait_ge(arg_done, 4 * i + su)
                            start = s_sum[:, 0, 0:1] if slot else total[:, su // 2:su // 2 + 1]
                            ve.tensor_tensor_scan(s_sum[:, slot, ::-1], e_buf[:, u % 2, ::-1], relu_s[:, slot, ::-1], start,
                                                  ALU.add, ALU.add).then_inc(sp_done, 1)
                            ve.wait_ge(sp_done, NU * i + u + 1)
                            ve.tensor_tensor(relu_s[:, slot, :], ps[:, u % 4, :], s_sum[:, slot, :],
                                             ALU.subtract).then_inc(arg_done, 1)

                        neg_abs(0)
                        for u in range(NU):
                            if u == 0:
                                aux(i, 2, v_t[:, HALF:], None, HALF)
                            if u == 1:
                                if begun:
                                    finish(i - 1)
                                    ve.wait_ge(kv_stored, 64 * i)
                                aux(i, 3, k_tok[:, 4, :], None, P)
                            if u == 2:
                                aux(i, 4, v_tok[:, 4, :], None, P)
                            if u + 1 in SAMPLE_AT:
                                su = SAMPLE_AT.index(u + 1)
                                for j in (1, 3):
                                    aux(i, keys_uses(1, su) - 2 + j // 2, kc_t[:, j], tiled=True)
                            if u == 3:
                                aux(i, TOTALS_USE, total[:, 0:2], None, 2)
                            if u + 1 < NU:
                                neg_abs(u + 1)
                            if UNITS[u][0] == "p":
                                softplus(u)
                            else:
                                suffix(u)
                            if u in CONVERT_AT and not last:
                                next_cvt(st, i, CONVERT_AT.index(u), last)
                        if not last:
                            evac_q(i + 1)
                            aux(i + 1, 1, k_t[:, HALF:], None, HALF)

                    ve.wait_ge(q_blk_zero, 1)
                    evac_q(0)
                    aux(0, 1, k_t[:, HALF:], None, HALF)
                    pair_of_heads(0, False, False)
                    with ve.Fori(1, PAIRS - 1) as i:
                        pair_of_heads(i, True, False)
                    pair_of_heads(PAIRS - 1, True, True)
                    finish(PAIRS - 1)
                    for c in range(DC):
                        ve.wait_ge(x_hi_done, b["x_hi"] + c + 1)
                        ve.tensor_tensor(xt_lo[:, c, :], o_t[:, c, :], xt_hi[:, c, :].bitcast(F32),
                                         ALU.subtract).then_inc(x_lo_done, 1)
                    for s in range(2):
                        next_cvt(st, PAIRS - 1, s, True)

        @block.tensor
        def _(pe):
            def products(s, chunks, x_hi, x_lo, bank, first=True, last=True, only=(0, 1)):
                n = len(chunks)
                for j, (cw, cx) in enumerate(chunks):
                    for w, xx in ((w_hi, x_hi), (w_hi, x_lo), (w_lo, x_hi)):
                        for half in only:
                            ins = pe.matmul(ps[:, bank[half], 0:HALF], w[:, s, cw, :],
                                            xx(cx, half), start=(first and j == 0 and w is w_hi and xx is x_hi),
                                            stop=(last and j == n - 1 and w is w_lo), skip_group_check=True)
                return ins

            def moving(t):
                return lambda c, half: t[:, c, half * HALF:(half + 1) * HALF]

            same = lambda n: [(c, c) for c in range(n)]

            def gate_or_up(st, s, only=(0, 1)):
                own = (p_hi, p_lo) if s and st.what == "ple" else (xt_hi, xt_lo)
                return products(s, same(st.chunks[s]), moving(own[0]), moving(own[1]), (2 * s, 2 * s + 1), only=only)

            def starts_early(st):
                return st.kind == "pair" and stages[stages.index(st) - 1].what == "norm"

            pe.wait_ge(const_step, 5)
            pe.wait_ge(const_r, 1)

            for st in stages:
                b = st.base
                if st.kind == "norm":
                    if st.what == "norm":
                        after(pe, evac_act, b["evac_act"])
                        after(pe, evac_dve, b["evac_dve"])
                        after(pe, prod_done, b["prod_done"])
                        after(pe, res_step, b["res_step"])
                    nxt = (stages + [None])[stages.index(st) + 1]
                    early = nxt is not None and starts_early(nxt)
                    banks_read, read = (res_done, "res_done") if adds_late(st) else (x_hat_done, "x_hat")
                    for t in range(TILES + 2):
                        if t < TILES and st.what == "norm":
                            if t >= 2:
                                pe.wait_ge(banks_read, b[read] + t - 1)
                            bank = 2 * (t % 2)
                            for c in range(DC):
                                ins = pe.transpose(ps[:, bank + c // 4, (c % 4) * P:(c % 4 + 1) * P],
                                                   y_t[:, c, t * P:(t + 1) * P], ident[:])
                            ins.then_inc(yt_full, 1)
                        if t >= 2 and st.then != "none":
                            n = t - 2
                            if early and n == TILES - 1:
                                pe.wait_ge(x_lo_done, b["x_lo"] + 3)
                                after(pe, banks_read, b[read] + (TILES if st.what == "norm" else 0))
                                pe.wait_ge(w_split, nxt.base["w"] + 1)
                                gate_or_up(nxt, 0, only=(0,))
                            if st.what == "norm":
                                pe.wait_ge(x_norm, b["x_norm"] + n + 1)
                            elif n == 0:
                                pe.wait_ge(x_loaded, 16 * TILES)
                            if n >= 2:
                                pe.wait_ge(x_lo_done, b["x_lo"] + n - 1)
                            if n == 0 and st.then == "window":
                                pe.wait_ge(band_step, 6)
                                pe.wait_ge(state_loaded, 16)
                            bank = 4 + 2 * (n % 2)
                            for c in range(DC):
                                out = ps[:, bank + c // 4, (c % 4) * P:(c % 4 + 1) * P]
                                chunk = slice(c * P, (c + 1) * P)
                                if st.then == "split":
                                    ins = pe.transpose(out, x[:, n, chunk], ident[:])
                                    continue
                                window = c * len(WINDOWS) // DC
                                kind = 2 if n == PROMPT_TILES else min(n, 1)
                                ins = pe.matmul(out, x[:, n, chunk], band[:, window, kind, :], start=(c % 4 == 0),
                                                stop=True, skip_group_check=True)
                                if kind == 2:
                                    ins = pe.matmul(out, state_t[:, chunk], band_state[0:DEC_BATCH * PREV, window, :],
                                                    start=False, stop=True, skip_group_check=True)
                                elif n:
                                    ins = pe.matmul(out[:, 0:PREV], x[96:P, n - 1, chunk], band_prev[96:P, window, 0:PREV],
                                                    start=False, stop=True, skip_group_check=True)
                            ins.then_inc(xt_full, 1)
                            if early and n == TILES - 1:
                                pe.wait_ge(w_split, nxt.base["w"] + 2)
                                gate_or_up(nxt, 1, only=(0,))
                elif st.kind == "ple":
                    pe.wait_ge(p_loaded, 32 * (st.layer + 1))
                    after(pe, evac_act, b["evac_act"])
                    after(pe, evac_dve, b["evac_dve"])
                    after(pe, x_lo_done, b["x_lo"])
                    for c in range(PLE // P):
                        for t in range(TILES):
                            ins = pe.transpose(ps[:, 4 + 2 * c + t // 4, (t % 4) * P:(t % 4 + 1) * P],
                                               p_tok[:, t, c * P:(c + 1) * P], ident[:])
                        ins.then_inc(pt_full, 1)
                elif st.kind == "pair":
                    after(pe, x_lo_done, b["x_lo"])
                    if st.what == "ple":
                        after(pe, pt_lo_done, b["pt_lo"])

                    early = starts_early(st)

                    def pair(i, begun):
                        only = (1,) if early and isinstance(i, int) else (0, 1)
                        pe.wait_ge(w_split, b["w"] + 2 * i + 1)
                        if begun:
                            pe.wait_ge(act_done, b["act_done"] + i)
                        gate_or_up(st, 0, only).then_inc(gate_full, 1)
                        pe.wait_ge(w_split, b["w"] + 2 * i + 2)
                        if begun:
                            pe.wait_ge(prod_done, b["prod_done"] + i)
                        gate_or_up(st, 1, only).then_inc(up_full, 1)

                    pair(0, b["act_done"] > 0)
                    with pe.Fori(1, st.pairs) as i:
                        pair(i, True)
                elif st.kind == "tile":
                    if st.what != "down":
                        after(pe, x_lo_done, b["x_lo"])
                    after(pe, evac_act, b["evac_act"])
                    after(pe, evac_dve, b["evac_dve"])
                    free = evac_dve if st.half else evac_act
                    base = b["evac_dve"] if st.half else b["evac_act"]
                    after(pe, pt_lo_done, b["pt_lo"])

                    def tiles(i, begun):
                        for s in range(2):
                            if begun:
                                pe.wait_ge(free, base + 2 * i + s - 1)
                            pe.wait_ge(w_split, b["w"] + 2 * i + s + 1)
                            bank = (4 + 2 * s, 5 + 2 * s)
                            if st.what == "down" and not begun and s == 0:
                                pe.wait_ge(h_lo_done, b["h_lo"] - 1)
                                products(s, same(FH - 1), moving(h_hi), moving(h_lo), bank, last=False)
                                pe.wait_ge(h_lo_done, b["h_lo"])
                                ins = products(s, [(FH - 1, FH - 1)], moving(h_hi), moving(h_lo), bank, first=False)
                            elif st.what == "down":
                                ins = products(s, same(FH), moving(h_hi), moving(h_lo), bank)
                            elif st.what == "out":
                                ins = products(s, same(DC), moving(xt_hi), moving(xt_lo), bank)
                            else:
                                def of(t):
                                    return lambda c, half: t[:, bass.ds(2 * i + c, 1), half * HALF:(half + 1) * HALF]
                                ins = products(s, same(2), of(h_hi), of(h_lo), bank)
                            ins.then_inc(acc_full, 1)
                    tiles(0, False)
                    with pe.Fori(1, DC // 2) as i:
                        tiles(i, True)
                elif st.kind == "attention":
                    after(pe, x_lo_done, b["x_lo"])
                    after(pe, evac_dve, b["evac_dve"])
                    attend(pe, st, products, moving)

_INS = ["x_prompt", "x_sample", "cache_k", "cache_v", "state_pool", "p_prompt", "p_sample", "ln_g", "ln_b", "ffn_w1",
        "ffn_w3", "ffn_w2", "pool_w", "pool_scale", "sb_w_in", "sb_w_out", "ple_w_gate", "ple_b_gate", "ple_w_proj"]
_OUTS = [(1, SEQ, D_MODEL), (DEC_BATCH, DEC_SEQ, D_MODEL), (1, 1, SEQ, HEADS, HEAD_DIM), (1, 1, SEQ, HEADS, HEAD_DIM),
         (1, DEC_BATCH, DEC_SEQ, HEADS, HEAD_DIM), (1, DEC_BATCH, DEC_SEQ, HEADS, HEAD_DIM), (1, 1, PREV, D_MODEL),
         (1, DEC_BATCH, PREV, D_MODEL)]


def kernel(**inputs):
    import numpy as _np
    import concourse.bacc as _bacc
    from concourse import mybir as _mybir
    from concourse.bass_utils import run_bass_kernel_spmd as _run

    nc = _bacc.Bacc("TRN2", target_bir_lowering=False, num_devices=1)
    arrays, args = {}, []
    for name in _INS:
        a = _np.ascontiguousarray(inputs[name])
        arrays[f"in_{name}_dram"] = a
        args.append(nc.dram_tensor(f"in_{name}_dram", a.shape, _mybir.dt.from_np(a.dtype), kind="ExternalInput").ap())
    for n, shape in enumerate(_OUTS):
        args.append(nc.dram_tensor(f"out_{n}_dram", shape, _mybir.dt.float32, kind="ExternalOutput").ap())
    streaming_trunk(nc, *args)
    r = _run(nc, [arrays], core_ids=[0])
    return tuple(r.results[0][f"out_{n}_dram"] for n in range(len(_OUTS)))
```
